# Optimizing a Trainium2 kernel written in Bass

```python
import math
import jax
import jax.numpy as jnp
from jax import lax
import numpy as np

D_MODEL = 2048
BATCH = 1
SEQ = 256
DEPTH = 2
DEC_BATCH = 8
DEC_SEQ = 4
PAST_LEN = 2048
PAGE_SIZE = 128

N_MIXERS = 2
HEAD_SIZE = 64
N_HEADS = D_MODEL // HEAD_SIZE
DECAY_LORA = max(32, int(round(D_MODEL ** 0.5 * 1.8 / 32)) * 32)
AAA_LORA = max(32, int(round(D_MODEL ** 0.5 * 1.8 / 32)) * 32)
MV_LORA = max(32, int(round(D_MODEL ** 0.5 * 1.3 / 32)) * 32)
GATE_LORA = max(32, int(round(D_MODEL ** 0.8 * 0.6 / 32)) * 32)
GN_EPS = 64e-5
LN_EPS = 1e-5
POOL_WINDOWS = (2, 4, 8, 16)
POOL_GROUPS = len(POOL_WINDOWS)
POOL_GROUP_WIDTH = D_MODEL // POOL_GROUPS
POOL_BUF = max(POOL_WINDOWS) - 1
D_FF = int(math.ceil(8 * D_MODEL / 3 / 256)) * 256
ALPHA = (2 * DEPTH) ** 0.25
BETA = (8 * DEPTH) ** -0.25
N_RWKV = (DEPTH + N_MIXERS - 1) // N_MIXERS
N_POOL = DEPTH // N_MIXERS

kernel_name = "rwkv7_pool_interleaved_deepnorm_step"

def _layer_norm(x, g, b):
    xf = x.astype(jnp.float32)
    mu = jnp.mean(xf, axis=-1, keepdims=True)
    var = jnp.mean(jnp.square(xf - mu), axis=-1, keepdims=True)
    return ((xf - mu) * lax.rsqrt(var + LN_EPS) * g.astype(jnp.float32) + b.astype(jnp.float32)).astype(x.dtype)

def _wkv_step(S, inp):
    r_t, w_t, k_t, v_t, a_t, b_t = inp
    Sa = jnp.einsum('bhvk,bhk->bhv', S, a_t)
    S = S * w_t[:, :, None, :] + Sa[..., None] * b_t[:, :, None, :] + v_t[..., None] * k_t[:, :, None, :]
    y = jnp.einsum('bhvk,bhk->bhv', S, r_t)
    return S, y

def _rwkv7_mix(x, shift_prev, wkv_prev, v_first, mu, w_r, w_k, w_v, w_o, w0, w1, w2,
               a0, a1, a2, g1, g2, k_k, k_a, r_k, gn_g, gn_b, vres):
    B, T, D = x.shape
    H, N = N_HEADS, HEAD_SIZE
    f32 = jnp.float32
    x_prev = jnp.concatenate([shift_prev[:, None, :].astype(x.dtype), x[:, :-1]], axis=1)
    xx = x_prev - x
    xr = x + xx * mu[0]
    xw = x + xx * mu[1]
    xk = x + xx * mu[2]
    xv = x + xx * mu[3]
    xa = x + xx * mu[4]
    xg = x + xx * mu[5]
    r = xr @ w_r
    w_log = -jax.nn.softplus(-(w0 + jnp.tanh(xw @ w1) @ w2).astype(f32)) - 0.5
    decay = jnp.exp(-jnp.exp(w_log))
    k = xk @ w_k
    v = xv @ w_v
    if vres is None:
        v_first = v
    else:
        v0, v1, v2 = vres
        v = v + (v_first - v) * jax.nn.sigmoid(v0 + (xv @ v1) @ v2)
    a = jax.nn.sigmoid(a0 + (xa @ a1) @ a2)
    g = jax.nn.sigmoid(xg @ g1) @ g2
    kk = (k * k_k).astype(f32).reshape(B, T, H, N)
    kk = kk / jnp.maximum(jnp.sqrt(jnp.sum(kk * kk, axis=-1, keepdims=True)), 1e-12)
    k = k * (1 + (a - 1) * k_a)

    def heads(z):
        return z.astype(f32).reshape(B, T, H, N)

    r_h, k_h, v_h, a_h = heads(r), heads(k), heads(v), heads(a)
    xs = tuple(jnp.swapaxes(z, 0, 1) for z in (r_h, heads(decay), k_h, v_h, -kk, kk * a_h))
    S_last, ys = lax.scan(_wkv_step, wkv_prev.astype(f32), xs)
    y = jnp.swapaxes(ys, 0, 1)
    ym = jnp.mean(y, axis=-1, keepdims=True)
    yv = jnp.mean(jnp.square(y - ym), axis=-1, keepdims=True)
    y = ((y - ym) * lax.rsqrt(yv + GN_EPS)).reshape(B, T, D) * gn_g.astype(f32) + gn_b.astype(f32)
    bonus = jnp.sum(r_h * k_h * r_k.astype(f32), axis=-1, keepdims=True) * v_h
    y = (y + bonus.reshape(B, T, D)).astype(x.dtype)
    out = (y * g) @ w_o
    return out, x[:, -1], S_last, v_first

def _pool_mix(x, past, start_pos, w_grp, scale):
    B, T, D = x.shape
    f32 = jnp.float32
    ext = jnp.concatenate([past.astype(x.dtype), x], axis=1)
    ext32 = ext.astype(f32)
    cs = jnp.concatenate([jnp.zeros((B, 1, D), f32), jnp.cumsum(ext32, axis=1)], axis=1)
    end = cs[:, POOL_BUF + 1:]
    pos = start_pos + jnp.arange(T)
    outs = []
    for gi, win in enumerate(POOL_WINDOWS):
        sl = slice(gi * POOL_GROUP_WIDTH, (gi + 1) * POOL_GROUP_WIDTH)
        lo = POOL_BUF + 1 - win
        start = cs[:, lo:lo + T, sl]
        cnt = jnp.minimum(win, pos + 1).astype(f32)[None, :, None]
        pooled = (end[..., sl] - start) / cnt
        outs.append(pooled - ext32[:, POOL_BUF:, sl])
    d = jnp.stack(outs, axis=2).astype(x.dtype)
    y = jnp.einsum('btgi,gio->btgo', d, w_grp).reshape(B, T, D)
    return y * scale, ext[:, -POOL_BUF:]

def _swiglu(x, w_in, w_down):
    h = x @ w_in
    gate, up = h[..., :D_FF], h[..., D_FF:]
    return (jax.nn.silu(gate) * up) @ w_down

def _trunk(x, wkv_st, shift_st, pool_st, start_pos, params):
    (ln_g, ln_b, rw_mu, rw_wr, rw_wk, rw_wv, rw_wo, rw_w0, rw_w1, rw_w2,
     rw_a0, rw_a1, rw_a2, rw_v0, rw_v1, rw_v2, rw_g1, rw_g2, rw_kk, rw_ka, rw_rk,
     rw_gn_g, rw_gn_b, pool_w, pool_scale, ffn_w_in, ffn_w_down) = params
    v_first = None
    new_wkv, new_shift, new_pool = [], [], []
    for i in range(DEPTH):
        j = i // N_MIXERS
        if i % N_MIXERS == 0:
            vres = None if j == 0 else (rw_v0[j - 1], rw_v1[j - 1], rw_v2[j - 1])
            h, sh, S, v_first = _rwkv7_mix(
                x, shift_st[j], wkv_st[j], v_first, rw_mu[j], rw_wr[j], rw_wk[j], rw_wv[j], rw_wo[j],
                rw_w0[j], rw_w1[j], rw_w2[j], rw_a0[j], rw_a1[j], rw_a2[j], rw_g1[j], rw_g2[j],
                rw_kk[j], rw_ka[j], rw_rk[j], rw_gn_g[j], rw_gn_b[j], vres)
            new_wkv.append(S)
            new_shift.append(sh)
        else:
            h, buf = _pool_mix(x, pool_st[j], start_pos, pool_w[j], pool_scale[j])
            new_pool.append(buf)
        x = _layer_norm(ALPHA * x + h, ln_g[i, 0], ln_b[i, 0])
        x = _layer_norm(ALPHA * x + _swiglu(x, ffn_w_in[i], ffn_w_down[i]), ln_g[i, 1], ln_b[i, 1])
    return x, jnp.stack(new_wkv), jnp.stack(new_shift), jnp.stack(new_pool)

def setup_inputs(seed: int = 0) -> dict:
    key = jax.random.key(seed)
    ks = iter(jax.random.split(key, 40))
    nrm = lambda shape, s: jax.random.normal(next(ks), shape, jnp.float32) * s
    D, H, N = D_MODEL, N_HEADS, HEAD_SIZE
    G, W = POOL_GROUPS, POOL_GROUP_WIDTH
    nv = max(N_RWKV - 1, 1)
    return {
        "x_prompt": nrm((BATCH, SEQ, D), 1.0),
        "x_sample": nrm((DEC_BATCH, DEC_SEQ, D), 1.0),
        "state_wkv": nrm((N_RWKV, DEC_BATCH, H, N, N), 0.3),
        "state_shift": nrm((N_RWKV, DEC_BATCH, D), 1.0),
        "state_pool": nrm((N_POOL, DEC_BATCH, POOL_BUF, D), 1.0),
        "ln_g": 1.0 + nrm((DEPTH, 2, D), 0.05),
        "ln_b": nrm((DEPTH, 2, D), 0.02),
        "rw_mu": jax.random.uniform(next(ks), (N_RWKV, 6, D), jnp.float32),
        "rw_wr": nrm((N_RWKV, D, D), D ** -0.5),
        "rw_wk": nrm((N_RWKV, D, D), D ** -0.5),
        "rw_wv": nrm((N_RWKV, D, D), D ** -0.5),
        "rw_wo": nrm((N_RWKV, D, D), D ** -0.5 * BETA),
        "rw_w0": jax.random.uniform(next(ks), (N_RWKV, D), jnp.float32, -3.0, 1.0),
        "rw_w1": nrm((N_RWKV, D, DECAY_LORA), D ** -0.5),
        "rw_w2": nrm((N_RWKV, DECAY_LORA, D), 0.1 * DECAY_LORA ** -0.5),
        "rw_a0": nrm((N_RWKV, D), 0.1),
        "rw_a1": nrm((N_RWKV, D, AAA_LORA), D ** -0.5),
        "rw_a2": nrm((N_RWKV, AAA_LORA, D), 0.3 * AAA_LORA ** -0.5),
        "rw_v0": nrm((nv, D), 0.1),
        "rw_v1": nrm((nv, D, MV_LORA), D ** -0.5),
        "rw_v2": nrm((nv, MV_LORA, D), 0.3 * MV_LORA ** -0.5),
        "rw_g1": nrm((N_RWKV, D, GATE_LORA), D ** -0.5),
        "rw_g2": nrm((N_RWKV, GATE_LORA, D), GATE_LORA ** -0.5),
        "rw_kk": 0.85 + nrm((N_RWKV, D), 0.05),
        "rw_ka": 1.0 + nrm((N_RWKV, D), 0.05),
        "rw_rk": nrm((N_RWKV, H, N), 0.1),
        "rw_gn_g": 1.0 + nrm((N_RWKV, D), 0.05),
        "rw_gn_b": nrm((N_RWKV, D), 0.02),
        "pool_w": nrm((N_POOL, G, W, W), W ** -0.5 * BETA),
        "pool_scale": 1.0 + nrm((N_POOL, D), 0.1),
        "ffn_w_in": nrm((DEPTH, D, 2 * D_FF), D ** -0.5),
        "ffn_w_down": nrm((DEPTH, D_FF, D), D_FF ** -0.5 * BETA),
    }

def reference(x_prompt, x_sample, state_wkv, state_shift, state_pool,
              ln_g, ln_b, rw_mu, rw_wr, rw_wk, rw_wv, rw_wo, rw_w0, rw_w1, rw_w2,
              rw_a0, rw_a1, rw_a2, rw_v0, rw_v1, rw_v2, rw_g1, rw_g2, rw_kk, rw_ka, rw_rk,
              rw_gn_g, rw_gn_b, pool_w, pool_scale, ffn_w_in, ffn_w_down):
    params = (ln_g, ln_b, rw_mu, rw_wr, rw_wk, rw_wv, rw_wo, rw_w0, rw_w1, rw_w2,
              rw_a0, rw_a1, rw_a2, rw_v0, rw_v1, rw_v2, rw_g1, rw_g2, rw_kk, rw_ka, rw_rk,
              rw_gn_g, rw_gn_b, pool_w, pool_scale, ffn_w_in, ffn_w_down)
    Bp = x_prompt.shape[0]
    wkv0 = jnp.zeros((N_RWKV, Bp, N_HEADS, HEAD_SIZE, HEAD_SIZE), jnp.float32)
    shift0 = jnp.zeros((N_RWKV, Bp, D_MODEL), x_prompt.dtype)
    pool0 = jnp.zeros((N_POOL, Bp, POOL_BUF, D_MODEL), x_prompt.dtype)
    y_prompt, wkv_p, shift_p, pool_p = _trunk(x_prompt, wkv0, shift0, pool0, 0, params)
    y_sample, wkv_s, shift_s, pool_s = _trunk(x_sample, state_wkv, state_shift, state_pool, PAST_LEN, params)
    return (y_prompt, y_sample, wkv_p, shift_p, pool_p, wkv_s, shift_s, pool_s)


_drawn_inputs = setup_inputs


def setup_inputs(seed=0):
    import zlib

    import numpy as np

    out = dict(_drawn_inputs(seed))
    spreads = {}
    factors = {'rw_w1': 5.821, 'rw_w2': 5.273, 'rw_kk': 12.206, 'rw_gn_g': 5.953, 'rw_gn_b': 21.806}
    for name, (base, spread) in spreads.items():
        noise = np.random.default_rng([zlib.crc32(name.encode()), seed]).standard_normal(out[name].shape)
        drawn = base * np.exp(spread * noise) if base else spread * noise
        out[name] = jnp.asarray(drawn.astype(out[name].dtype))
    for name, factor in factors.items():
        out[name] = (out[name] * factor).astype(out[name].dtype)
    return out
```

```python
from contextlib import ExitStack

import numpy as np

import concourse.bass as bass
from concourse import mybir

F32 = mybir.dt.float32
F32R = mybir.dt.float32r
ACT = mybir.ActivationFunctionType
ALU = mybir.AluOpType

D = 2048
SEQ = 256
NSEQ, NSTEP = 8, 4
NS = NSEQ * NSTEP
T = SEQ + NS
HN = 64
H = D // HN
FF = 5632
P = 128
KC = D // P
FC = FF // P
HG = FC // 2
HH2 = HG // 2
DL = 96
GL = 256
BUF = 15
ALPHA = 4.0 ** 0.25
LN_EPS = 1e-5
GN_EPS = 64e-5
DECAY = -float(np.exp(-0.5))
CH = 64

SLAB = dict(lora1=0, r=4, k=20, v=36, lora2=52, g2=54, o=56, ffn0=72, pool=224, ffn1=228)
OUT = dict(lora1=0, r=4, k=20, v=36, lora2=52, g2=84, o=100, ffn0=116, pool=236, ffn1=252)
ROW = dict(lora2=0, g2=32, pool=48)
FFN_SLABS, FFN_OUTS = 76, 60
MIX = dict(w=0, a=1, g=2, r=3, k=4, v=5)
MU_ROW = dict(r=0, w=1, k=2, v=3, a=4, g=5)

PCOL = dict(w0=96, a0=112, k_k=128, k_a=144, r_k=160, gn_g=176, gn_b=192, scale=208, ln_g=256, ln_b=320)


def shape_constants():
    i = np.arange(P)[:, None]
    j = np.arange(P)[None, :]
    same = (i // CH) == (j // CH)
    cols = [np.eye(P), np.full((P, P), 1.0 / D), same, same / HN]
    perm = np.concatenate([c.astype(np.float32) for c in cols], 1)

    def level(n, m):
        a, b = np.arange(n)[:, None], np.arange(n)[None, :]
        return (a // (2 * m) == b // (2 * m)) & (a // m % 2 == 1) & (b // m % 2 == 0)

    t4 = np.arange(NS)
    s4 = (t4[:, None] // NSTEP) == (t4[None, :] // NSTEP)
    up, upi = t4[:, None] < t4[None, :], t4[:, None] <= t4[None, :]
    notstart = np.ones(T)
    notstart[0:SEQ:CH] = 0
    notstart[SEQ::NSTEP] = 0
    wkv = [same & (i < j), same & (i <= j)] + [level(P, m) for m in (2, 4, 8, 16, 32)] + [level(P, 1).T]
    wkv += [np.tile(s4 & up, (4, 1)), np.tile(s4 & upi, (4, 1)), np.tile(level(NS, 1).T, (4, 1)),
            np.tile(level(NS, 2), (4, 1)), np.tile(np.eye(NS), (4, 1)),
            np.tile(t4[:, None] // NSTEP == np.arange(NSEQ)[None, :], (4, 1)), np.tile(notstart, (P, 1))]
    wkv = np.concatenate([c.astype(np.float32) for c in wkv], 1)
    inv = np.ones((4, 16), np.float32)
    for g in range(4):
        w = 2 << g
        inv[g] = w / np.minimum(w, np.arange(16) + 1).astype(np.float32)
    return perm, wkv, np.tile(inv.reshape(1, 64), (P, 1)).astype(np.float32)


NW = 256 + 5 * 128 + 128 + 64 + 32 * 3 + 8 + T


class Chain:

    def __init__(self, eng, sem, per=0):
        self.eng, self.sem, self.per, self.i, self.n = eng, sem, per, 0, 0

    def turn(self, i):
        assert self.per == 0 or self.n in (0, self.per), self.n
        self.i, self.n = i, 0

    def __call__(self, ins):
        self.n += 1
        ins.then_inc(self.sem, 1)
        self.eng.wait_ge(self.sem, self.i * self.per + self.n)


def build(nc, x_prompt, x_sample, state_wkv, state_shift, state_pool, ln_g, ln_b, rw_mu, rw_wr, rw_wk, rw_wv,
          rw_wo, rw_w0, rw_w1, rw_w2, rw_a0, rw_a1, rw_a2, rw_g1, rw_g2, rw_kk, rw_ka, rw_rk, rw_gn_g, rw_gn_b,
          pool_w, pool_scale, ffn_w_in, ffn_w_down, c_perm, c_wkv, c_inv,
          y_prompt, y_sample, wkv_p, shift_p, pool_p, wkv_s, shift_s, pool_s):
    ctx = ExitStack()
    with ctx:
        base = (nc.sbuf_base + 31) // 32 * 32
        place = {}

        def at(name, shape, dt, offset):
            n = 4
            for s in shape[1:]:
                n *= s
            place[name] = (offset, offset + n)
            return nc.alloc_sbuf_tensor_at(name, shape, dt, offset=base + offset)

        def after(name):
            return place[name][1]

        def sem(name):
            return ctx.enter_context(nc.semaphore(name))

        RAW = at("RAW", [P, 4, 2048], F32, 0)
        WH = at("WH", [P, 2, 2048], F32R, after("RAW"))
        WL = at("WL", [P, 2, 2048], F32R, after("WH"))
        X = at("X", [P, KC, T + 1], F32, after("WL"))
        XPS = at("XPS", [P, KC, NS], F32, after("X"))
        PAR = at("PAR", [P, 3 * P], F32, after("XPS"))
        OMU = at("OMU", [P, 96], F32, after("PAR"))
        CP = at("CP", [P, 4 * P], F32, after("OMU"))
        TM = at("TM", [P, 2, T], F32, after("CP"))
        LHH = at("LHH", [P, 4, T], F32R, after("TM"))
        LHL = at("LHL", [P, 4, T], F32R, after("LHH"))
        MH = [None, None]
        ML = [None, None]
        MH[0] = at("MH0", [P, KC, T], F32R, after("LHL"))
        ML[0] = at("ML0", [P, KC, T], F32R, after("MH0"))
        MH[1] = at("MH1", [P, KC, T], F32R, after("ML0"))
        ML[1] = at("ML1", [P, KC, T], F32R, after("MH1"))
        R = at("R", [P, KC, T], F32, after("ML1"))
        K = at("K", [P, KC, T], F32, after("R"))
        assert base + after("K") <= nc.sbuf_usable_end, (base, after("K"), nc.sbuf_usable_end)
        XROW = at("XROW", [P, 2, 3, 512], F32, place["MH1"][0])
        PROW = at("PROW", [P, 3, P], F32, after("XROW"))
        V = at("V", [P, KC, T], F32, place["MH0"][0])
        SG = at("SG", [P, KC, T], F32, place["ML1"][0])
        A = at("A", [P, KC, T], F32, place["MH1"][0])
        KK = at("KK", [P, KC, T], F32, place["ML0"][0])
        off = [0]

        def ring(name, shape, dt=F32):
            t = at(name, shape, dt, off[0])
            off[0] = (place[name][1] + 31) // 32 * 32
            assert off[0] <= place["X"][0]
            return t

        CW = ring("CW", [P, NW])
        S0N = ring("S0N", [P, 4, P])
        S0T = ring("S0T", [P, NSEQ, HN])
        AR = ring("AR", [P, 2, T])
        BF = ring("BF", [P, T])
        KF = ring("KF", [P, T])
        VF = ring("VF", [P, T])
        CS = ring("CS", [P, T])
        CSX = ring("CSX", [P, T])
        PC = ring("PC", [P, T])
        IPC = ring("IPC", [P, T])
        PPC = ring("PPC", [P, T])
        RKP = ring("RKP", [P, T])
        KT = ring("KT", [P, T])
        TOK = ring("TOK", [P, 2, 4, P])
        TS = ring("TS", [P, 3, HN])
        LR = ring("LR", [P, 2, 2, 256])
        MR = ring("MR", [P, 2, 2, 256])
        SM = ring("SM", [P, 64])
        TI = ring("TI", [P, 4, P])
        TIT = ring("TIT", [P, 4, P])
        XL = ring("XL", [P, 4, P])
        STI = ring("STI", [P, NS])
        STT = ring("STT", [P, NS])
        SXL = ring("SXL", [P, NS])
        MV = ring("MV", [P, 4, HN])
        WT = ring("WT", [P, 2, P])
        Q = ring("Q", [P, 4, HN])
        WR = ring("WR", [P, NSEQ, 8])
        QT = ring("QT", [P, NS])
        MVS = ring("MVS", [P, HN])
        UT = ring("UT", [P, NS])
        U = ring("U", [P, 2, P])
        ST = ring("ST", [P, 2, HN])
        SPD = ring("SPD", [P, HN])
        UVX = ring("UVX", [P, NSEQ, HN])
        SNW = ring("SNW", [P, NSEQ, HN])
        SOS = ring("SOS", [P, 4, P])
        SOP = ring("SOP", [HN, P])
        YC = ring("YC", [P, T])
        YQ = ring("YQ", [P, T])
        YD = ring("YD", [P, T])
        YR = ring("YR", [P, T])
        hid = place["MH1"][0]
        HH = at("HH", [P, HG, T], F32R, hid)
        HL = at("HL", [P, HG, T], F32R, after("HH"))
        assert after("HL") <= after("K")
        SQ = at("SQ", [P, KC, T], F32, hid)
        LNS = at("LNS", [P, 2, T], F32, after("SQ"))
        EP = [at("EP0", [P, KC, BUF + SEQ], F32, hid)]
        EP.append(at("EP1", [P, KC, BUF + SEQ], F32, after("EP0")))
        ES1 = at("ES1", [P, KC, NSEQ, BUF + NSTEP], F32, after("EP1"))
        ES = [at("ES0", [P, KC, NSEQ, BUF + NSTEP], F32, after("ES1")), ES1]
        assert place["ES0"][0] >= after("LNS")
        CI = at("CI", [P, 4, 16], F32, after("ES0"))
        DP = at("DP", [P, KC, T], F32, after("CI"))
        PAST = at("PAST", [P, D], F32, place["DP"][0])
        assert after("DP") <= after("K")
        TR = at("TR", [48, D], F32, place["MH0"][0])
        YROW = at("YROW", [P, 3, D], F32, hid)

        PS = [ctx.enter_context(nc.psum_tensor(f"PS{i}", [P, 512], F32)) for i in range(8)]

        IDN = CP[:, 0:P]
        AVG = CP[:, P:2 * P]
        HEADS = CP[:, 2 * P:3 * P]
        HEADAVG = CP[:, 3 * P:4 * P]
        cm = [0]

        def cw(n):
            cm[0] += n
            return CW[:, cm[0] - n:cm[0]]

        M_PROD = cw(256)
        M_LEVEL = [cw(P) for _ in range(5)]
        M_ONE = cw(P)
        MS_PROD = cw(64)
        MS_ONE = cw(NS)
        MS_TWO = cw(NS)
        IDS = cw(NS)
        MS_SEQ = cw(NSEQ)
        NOTSTART = cw(T)
        assert cm[0] == NW

        def par(name, c):
            return PAR[:, bass.ds(PCOL[name] + c, 1)]

        const_in = sem("const_in")
        prow_in = sem("prow_in")
        xrow_in = [sem(f"xrow_in{i}") for i in range(2)]
        x_turned = sem("x_turned")
        x_bank_free = sem("x_bank_free")
        par_turned = sem("par_turned")
        par_ready = sem("par_ready")
        x_ready = sem("x_ready")
        omu_ready = sem("omu_ready")
        xps_ready = sem("xps_ready")
        raw_landed = [sem(f"raw_landed{i}") for i in range(4)]
        hi_ready = sem("hi_ready")
        lo_ready = sem("lo_ready")
        slab_used = sem("slab_used")
        row_ready = sem("row_ready")
        out_free = sem("out_free")
        tm_ready = sem("tm_ready")
        mt_ready = sem("mt_ready")
        mixhi_ready = sem("mixhi_ready")
        mixlo_ready = sem("mixlo_ready")
        lh_ready = sem("lh_ready")
        lhh_ready = sem("lhh_ready")
        lhl_ready = sem("lhl_ready")
        kc_ready = sem("kc_ready")
        kks_ready = sem("kks_ready")
        kkn_ready = sem("kkn_ready")
        kkd_ready = sem("kkd_ready")
        kk_ready = sem("kk_ready")
        kk_self = sem("kk_self")
        wkv_go = sem("wkv_go")
        wkv_const = sem("wkv_const")
        wkv_done = sem("wkv_done")
        yg_ready = sem("yg_ready")
        ygh_ready = sem("ygh_ready")
        ygl_ready = sem("ygl_ready")
        o_done = sem("o_done")
        sg_ready = sem("sg_ready")
        hid_ready = sem("hid_ready")
        hh_ready = sem("hh_ready")
        hl_ready = sem("hl_ready")
        act_self = sem("act_self")
        hid_self = sem("hid_self")
        stores = sem("stores")
        final_stores = sem("final_stores")

        w = {n: sem("w_" + n) for n in (
            "cs", "decays", "vcopy", "feats", "tokT", "tok", "prod", "prodm", "t2t", "t2", "t2c",
            "xmm", "xmask", "tmm", "tadd", "ttt", "ttc", "xf", "xfm", "ttf", "ttfin",
            "mv", "mvc", "q", "qc", "umm", "uadd", "smm", "snew", "spd", "ymm", "yout",
            "s0in", "s0t", "s0c", "wa", "ut", "utt", "utc", "uvx", "snmm", "snew2", "snt", "sos", "sop", "sopc",
            "rkp", "bon", "bonv", "ymean", "ycen", "ysq", "yvar", "ysd", "ydone", "self", "aself", "store", "s0free")}

        block = ctx.enter_context(nc.Block())

        @block.sync
        def _(sp):
            sp.dma_start(CP[:, :], c_perm).then_inc(const_in, 16)
            rows = lambda a: a.rearrange("(c p) -> c p", p=P)
            prow = [(0, 96, rw_mu.rearrange("n j (c p) -> (n j c) p", p=P)), (96, 16, rows(rw_w0[0])),
                    (112, 16, rows(rw_a0[0])), (128, 16, rows(rw_kk[0])), (144, 16, rows(rw_ka[0])),
                    (160, 16, rw_rk.rearrange("n (c e) v -> (n c) (e v)", e=2)), (176, 16, rows(rw_gn_g[0])),
                    (192, 16, rows(rw_gn_b[0])), (208, 16, rows(pool_scale[0])),
                    (256, 64, ln_g.rearrange("a b (c p) -> (a b c) p", p=P)),
                    (320, 64, ln_b.rearrange("a b (c p) -> (a b c) p", p=P))]
            for col, n, src in prow:
                sp.dma_start(PROW[col % P:col % P + n, col // P, :], src).then_inc(prow_in, 16)
            with sp.Fori(0, 2) as i:
                for b in range(2):
                    sp.wait_ge(x_turned, 8 * i + 4 * b + 4)
                    cols = bass.ds((2 * i + b) * 512, 512)
                    sp.dma_start(XROW[:, b, 0:2, :], x_prompt[0][:, cols].rearrange("(a p) n -> p a n", p=P))\
                      .then_inc(xrow_in[b], 16)
                    sp.dma_start(XROW[0:NS, b, 2, :], x_sample.rearrange("b t d -> (b t) d")[:, cols])\
                      .then_inc(xrow_in[b], 16)
                    sp.dma_start(XROW[NS:NS + NSEQ, b, 2, :], state_shift[0][:, cols]).then_inc(xrow_in[b], 16)

            def slab(s, slot, dst, src):
                sp.wait_ge(lo_ready, s + 1)
                sp.dma_start(dst, src).then_inc(raw_landed[slot], 16)

            def square(s0, wt):
                with sp.Fori(0, 4) as i:
                    for j in range(4):
                        slab(s0 + 4 * i + j, j, RAW[:, j, :].rearrange("p (k m) -> p k m", k=KC),
                             wt[:, bass.ds((4 * i + j) * P, P)].rearrange("(k p) m -> p k m", p=P))

            s = SLAB["lora1"]
            for j, src in enumerate((rw_w1[0], rw_a1[0])):
                slab(s + j, j, RAW[:, j, 0:KC * DL].rearrange("p (k m) -> p k m", k=KC),
                     src.rearrange("(k p) m -> p k m", p=P))
            for j in range(2):
                slab(s + 2 + j, 2 + j, RAW[:, 2 + j, :].rearrange("p (k m) -> p k m", k=KC),
                     rw_g1[0][:, j * P:(j + 1) * P].rearrange("(k p) m -> p k m", p=P))
            square(SLAB["r"], rw_wr[0])
            square(SLAB["k"], rw_wk[0])
            square(SLAB["v"], rw_wv[0])
            s = SLAB["lora2"]
            slab(s, 0, RAW[0:DL, 0, :], rw_w2[0])
            slab(s + 1, 1, RAW[0:DL, 1, :], rw_a2[0])

            sp.wait_ge(wkv_go, 2)
            sp.dma_start(CW[:, :], c_wkv).then_inc(wkv_const, 16)
            with sp.Fori(0, KC) as p:
                sp.wait_ge(w["s0t"], p + 1)
                for b2 in range(2):
                    for h in range(2):
                        src = state_wkv[0].rearrange("(b c) h v k -> c v b h k", c=2)[b2][:, :, bass.ds(2 * p + h, 1), :]
                        sp.dma_start(S0N[b2 * HN:(b2 + 1) * HN, :, h * HN:(h + 1) * HN],
                                     src.rearrange("v b h k -> v b (h k)")).then_inc(w["s0in"], 16)

            sp.wait_ge(wkv_done, 3)
            s = SLAB["g2"]
            for j in range(2):
                slab(s + j, 2 + j, RAW[:, 2 + j, :], rw_g2[0][j * P:(j + 1) * P, :])
            square(SLAB["o"], rw_wo[0])

            def ffn(layer):
                w_in = ffn_w_in[layer]
                w_down = ffn_w_down[layer]
                for g in range(2):
                    s = SLAB[f"ffn{layer}"] + g * FFN_SLABS
                    with sp.Fori(0, HG // 2) as i:
                        for j in range(4):
                            c = FC * (j % 2) + g * HG + 2 * i + j // 2
                            slab(s + 4 * i + j, j, RAW[:, j, :].rearrange("p (k m) -> p k m", k=KC),
                                 w_in[:, bass.ds(c * P, P)].rearrange("(k p) m -> p k m", p=P))
                    with sp.Fori(0, KC // 2) as i:
                        for j in range(4):
                            r0 = (g * HG + (j % 2) * HH2) * P
                            slab(s + 2 * HG + 4 * i + j, j,
                                 RAW[:, j, 0:HH2 * P].rearrange("p (k m) -> p k m", k=HH2),
                                 w_down[r0:r0 + HH2 * P, bass.ds((2 * i + j // 2) * P, P)]
                                 .rearrange("(k p) m -> p k m", p=P))

            ffn(0)
            for j in range(4):
                slab(SLAB["pool"] + j, j, RAW[:, j, :].rearrange("p (k m) -> p k m", k=4),
                     pool_w[0, j].rearrange("(k p) m -> p k m", p=P))
            ffn(1)

        past_go, past_in, inv_in, tr_ready = sem("past_go"), sem("past_in"), sem("inv_in"), sem("tr_ready")
        yrow_ready = sem("yrow_ready")

        @block.gpsimd
        def _(pool):
            pool.sem_inc(x_turned, 8)
            pool.sem_inc(x_bank_free, 4)
            pool.sem_inc(lo_ready, 4)
            pool.sem_inc(slab_used, 2)
            pool.sem_inc(out_free, 4)
            pool.sem_inc(mixlo_ready, 2)
            pool.sem_inc(hl_ready, 2)
            pool.sem_inc(w["s0t"], 1)
            pool.sem_inc(kk_ready, 2)
            pool.dma_start(shift_p[0], x_prompt[0, SEQ - 1:SEQ, :]).then_inc(stores, 16)
            pool.dma_start(shift_s[0], x_sample[:, NSTEP - 1, :]).then_inc(stores, 16)
            pool.dma_start(pool_s[0][:, 0:BUF - NSTEP, :], state_pool[0][:, NSTEP:BUF, :]).then_inc(stores, 16)
            with pool.Fori(0, KC) as p:
                pool.wait_ge(const_in, 16)
                pool.wait_ge(w["sopc"], p + 1)
                pool.dma_start(wkv_p[0, 0].rearrange("h v k -> v h k")[:, bass.ds(2 * p, 2), :],
                               SOP[:, :].rearrange("v (h k) -> v h k", h=2)).then_inc(w["store"], 16)
                pool.wait_ge(const_in, 16)
                pool.wait_ge(w["sos"], p + 1)
                for b2 in range(2):
                    for h in range(2):
                        dst = wkv_s[0].rearrange("(b c) h v k -> c v b h k", c=2)[b2][:, :, bass.ds(2 * p + h, 1), :]
                        pool.dma_start(dst.rearrange("v b h k -> v b (h k)"),
                                       SOS[b2 * HN:(b2 + 1) * HN, :, h * HN:(h + 1) * HN]).then_inc(w["store"], 16)
                pool.wait_ge(w["store"], 80 * p + 80)
                pool.sem_inc(w["s0free"], 1)
            pool.sem_inc(wkv_done, 1)
            pool.wait_ge(past_go, 2)
            pool.dma_start(PAST[0:NSEQ * BUF, :], state_pool[0].rearrange("b t d -> (b t) d")).then_inc(past_in, 16)
            pool.dma_start(CI[:, :, :], c_inv.rearrange("p (g t) -> p g t", g=4)).then_inc(inv_in, 16)
            pool.wait_ge(tr_ready, 4)
            pool.dma_start(pool_p[0, 0], TR[1:16, :]).then_inc(stores, 16)
            pool.dma_start(pool_s[0][:, BUF - NSTEP:BUF, :], TR[16:48, :]).then_inc(stores, 16)
            pool.wait_ge(stores, 16 * 5)
            pool.sem_inc(tr_ready, 1)
            pool.wait_ge(yrow_ready, 12)
            pool.dma_start(y_prompt[0].rearrange("(a p) d -> p a d", p=P), YROW[:, 0:2, :]).then_inc(final_stores, 16)
            pool.dma_start(y_sample.rearrange("b t d -> (b t) d"), YROW[0:NS, 2, :]).then_inc(final_stores, 16)
            pool.wait_ge(final_stores, 32)

        ln = {n: sem("ln_" + n) for n in ("x", "mean", "cen", "sq", "var", "sd", "rstd", "scaled", "done", "hi", "lo")}
        HALVED = {0: 0, 2: KC}
        pl = {n: sem("pool_" + n) for n in ("pastT", "past", "ext", "d", "hi", "lo", "scaled", "trT", "self")}
        yt = {n: sem("yt_" + n) for n in ("T", "free")}
        LAST = {"lora1": 2048, "r": 2048, "k": 2048}

        @block.tensor
        def _(pe):
            def three(out, wh, wl, xh, xl, first, last):
                pe.matmul(out, wh, xh, start=first, stop=False)
                pe.matmul(out, wh, xl, start=False, stop=False)
                return pe.matmul(out, wl, xh, start=False, stop=last)

            def take_slab(s):
                pe.wait_ge(lo_ready, s + 5)

            def take_bank(o):
                pe.wait_ge(out_free, o + 1)

            pe.wait_ge(const_in, 16)
            pe.wait_ge(prow_in, 16 * 11)
            for g, n in ((0, 128), (1, 96), (2, 128)):
                ins = pe.transpose(PS[4][:, g * P:g * P + n], PROW[0:n, g, :], CP[0:n, 0:n])
            ins.then_inc(par_turned, 1)
            with pe.Fori(0, 2) as i:
                for b in range(2):
                    pe.wait_ge(xrow_in[b], 48 * i + 48)
                    for c in range(4):
                        pe.wait_ge(x_bank_free, (2 * i + b) * 4 + c + 1)
                        for a, (n, m) in enumerate(((P, P), (P, P), (NS + NSEQ, NS + NSEQ))):
                            ins = pe.transpose(PS[c][:, a * P:a * P + n], XROW[0:n, b, a, c * P:(c + 1) * P],
                                               CP[0:n, 0:n])
                        ins.then_inc(x_turned, 1)

            for j, (name, wd) in enumerate((("w", DL), ("a", DL), ("g", P), ("g", P))):
                s, o = SLAB["lora1"] + j, OUT["lora1"] + j
                take_slab(s)
                take_bank(o)
                if j == 0:
                    pe.wait_ge(x_bank_free, 20)
                q, m = MIX[name], MIX[name] % 2
                for k in range(KC):
                    if j < 3:
                        pe.wait_ge(mixlo_ready, 2 + q * KC + k + 1)
                    ins = three(PS[o % 4][0:wd, 0:T], WH[:, s % 2, k * wd:(k + 1) * wd], WL[:, s % 2, k * wd:(k + 1) * wd],
                                MH[m][:, k, :], ML[m][:, k, :], k == 0, k == KC - 1)
                ins.then_inc(slab_used, 1)

            def square(name, xh, xl, extra=None):
                s0, o0 = SLAB[name], OUT[name]
                with pe.Fori(0, 4) as i:
                    for j in range(4):
                        take_slab(s0 + 4 * i + j)
                        take_bank(o0 + 4 * i + j)
                        for k in range(KC):
                            ins = three(PS[j][:, 0:T], WH[:, j % 2, k * P:(k + 1) * P], WL[:, j % 2, k * P:(k + 1) * P],
                                        xh[:, k, :], xl[:, k, :], k == 0, k == KC - 1)
                        ins.then_inc(slab_used, 1)
                        if extra is not None:
                            extra(i, j)

            for name in ("r", "k"):
                q = MIX[name]
                pe.wait_ge(mixlo_ready, 2 + (q + 1) * KC)
                square(name, MH[q % 2], ML[q % 2])

            def key_norms(i, j):
                pe.wait_ge(kks_ready, 4 * i + j + 1)
                pe.matmul(PS[4 + j % 2][:, 0:T], HEADS, TM[:, j % 2, :], start=True, stop=True).then_inc(kkn_ready, 1)

            pe.wait_ge(mixlo_ready, 2 + 6 * KC)
            square("v", MH[1], ML[1], key_norms)

            pe.wait_ge(lhl_ready, 4)
            for j in range(2):
                s = SLAB["lora2"] + j
                take_slab(s)
                for m in range(KC):
                    o = OUT["lora2"] + j * KC + m
                    take_bank(o)
                    ins = three(PS[o % 4][:, 0:T], WH[0:DL, j, m * P:(m + 1) * P], WL[0:DL, j, m * P:(m + 1) * P],
                                LHH[0:DL, j, :], LHL[0:DL, j, :], True, True)
                    ins.then_inc(row_ready, 1)
                pe.drain().then_inc(slab_used, 1)
            pe.sem_inc(wkv_go, 1)

            pe.wait_ge(wkv_const, 16)
            pe.wait_ge(out_free, 4 + OUT["g2"])
            hr = [slice(0, HN), slice(HN, P)]
            def lo32(h):
                return slice(h * HN, h * HN + 32)

            def hi32(h):
                return slice(h * HN + 32, h * HN + 64)

            def await_step(semaphore, value):
                pe.wait_ge(const_in, 16)
                pe.wait_ge(semaphore, value)

            with pe.Fori(0, KC) as p:
                await_step(w["s0in"], 64 * p + 64)
                await_step(w["ydone"], p + 1)
                for b in range(4):
                    ins = pe.transpose(PS[0][:, b * P:(b + 1) * P], S0N[:, b, :], IDN)
                ins.then_inc(w["s0t"], 1)
                await_step(w["feats"], p + 1)
                await_step(w["vcopy"], p + 1)
                feats = [AR[:, 0, :], BF[:, :], KF[:, :], VF[:, :]]
                for t in range(2):
                    for n, f in enumerate(feats):
                        ins = pe.transpose(PS[1 + t][:, n * P:(n + 1) * P], f[:, t * P:(t + 1) * P], IDN)
                for h in range(2):
                    for n, (f, z) in enumerate(((0, 0), (0, 1), (1, 0), (2, 1), (3, 0), (3, 1))):
                        ins = pe.matmul(PS[3][h * HN + 32 * z:h * HN + 32 * z + 32, (n // 2) * HN:(n // 2 + 1) * HN],
                                        feats[f][hr[h], SEQ:T], CP[hr[h], hr[h]], start=True, stop=True)
                ins.then_inc(w["tokT"], 1)
                for t in range(2):
                    for h in range(2):
                        ins = pe.matmul(PS[4 + h][:, t * 256:(t + 1) * 256], BF[hr[h], t * P:(t + 1) * P],
                                        AR[hr[h], :, t * P:(t + 1) * P], start=True, stop=True)
                    for h in range(2):
                        ins = pe.matmul(PS[6 + h][:, t * 256:(t + 1) * 256], KF[hr[h], t * P:(t + 1) * P],
                                        AR[hr[h], :, t * P:(t + 1) * P], start=True, stop=True)
                await_step(w["s0c"], p + 1)
                for h in range(2):
                    for z, f in ((0, BF), (1, KF)):
                        ins = pe.matmul(PS[0][h * HN + 32 * z:h * HN + 32 * z + 32, 0:64], f[hr[h], SEQ:T],
                                        AR[hr[h], :, SEQ:T], start=True, stop=True)
                ins.then_inc(w["prod"], 1)
                await_step(w["tok"], p + 1)
                await_step(w["t2t"], p + 1)
                for u in range(4):
                    pe.transpose(PS[1][:, u * P:(u + 1) * P], TIT[:, u, :], IDN)
                for h in range(2):
                    ins = pe.matmul(PS[2][lo32(h), 0:NS], STT[lo32(h), :], IDS[lo32(h), :], start=True, stop=True)
                ins.then_inc(w["t2"], 1)
                for lv in range(5):
                    await_step(w["t2c"] if lv == 0 else w["ttc"], p + 1 if lv == 0 else 4 * p + lv)
                    for u in range(4):
                        ins = pe.matmul(PS[3][:, u * P:(u + 1) * P], LR[:, u // 2, u % 2, 0:P], TI[:, u, :],
                                        start=True, stop=True)
                    if lv == 0:
                        for h in range(2):
                            ins = pe.matmul(PS[4][lo32(h), 0:NS], SM[lo32(h), 0:NS], STI[lo32(h), :],
                                            start=True, stop=True)
                    ins.then_inc(w["xmm"], 1)
                    await_step(w["xmask"], 5 * p + lv + 1)
                    if lv < 4:
                        for u in range(4):
                            ins = pe.matmul(PS[5][:, u * P:(u + 1) * P], TIT[:, u, :], XL[:, u, :],
                                            start=True, stop=True)
                        if lv == 0:
                            for h in range(2):
                                ins = pe.matmul(PS[4][lo32(h), 64:64 + NS], SXL[lo32(h), :], STT[lo32(h), :],
                                                start=True, stop=True)
                        ins.then_inc(w["tmm"], 1)
                        await_step(w["tadd"], 5 * p + lv + 1)
                        for u in range(4):
                            ins = pe.transpose(PS[6][:, u * P:(u + 1) * P], TI[:, u, :], IDN)
                        ins.then_inc(w["ttt"], 1)
                    else:
                        for u in range(4):
                            ins = pe.matmul(PS[5][:, u * P:(u + 1) * P], XL[:, u, :], TIT[:, u, :],
                                            start=True, stop=True)
                        ins.then_inc(w["tmm"], 1)
                for u in range(4):
                    t, h = u // 2, u % 2
                    ins = pe.matmul(PS[7][:, u * HN:(u + 1) * HN], MR[:, t, h, 0:P], TOK[:, t, 3, hr[h]],
                                    start=True, stop=True)
                for h in range(2):
                    ins = pe.matmul(PS[7][lo32(h), 256:256 + HN], SM[hi32(h), 0:NS], TS[hi32(h), 2, :],
                                    start=True, stop=True)
                ins.then_inc(w["mv"], 1)
                await_step(w["tadd"], 5 * p + 5)
                await_step(w["mvc"], p + 1)
                for u in range(4):
                    t, h = u // 2, u % 2
                    pe.matmul(PS[1][hr[h], t * P:(t + 1) * P], TOK[:, t, 0, hr[h]], TIT[:, u, :],
                              start=True, stop=True)
                for h in range(2):
                    pe.matmul(PS[1][hr[h], 256:256 + NS], TS[lo32(h), 0, :], STT[lo32(h), :], start=True, stop=True)
                for h in range(2):
                    pe.matmul(PS[1][hr[h], 320:320 + NS], MVS[lo32(h), :], STT[lo32(h), :], start=True, stop=True)
                for u in range(4):
                    ins = pe.matmul(PS[2][:, u * HN:(u + 1) * HN], TIT[:, u, :], MV[:, u, :], start=True, stop=True)
                ins.then_inc(w["q"], 1)
                await_step(w["rkp"], p + 1)
                pe.matmul(PS[3][:, 0:T], HEADS, RKP[:, :], start=True, stop=True).then_inc(w["bon"], 1)
                await_step(w["qc"], p + 1)
                for h in range(2):
                    for b in range(NSEQ):
                        ins = pe.matmul(PS[4][hr[h], b * 8:(b + 1) * 8], S0T[hr[h], b, :], WR[hr[h], b, :],
                                        start=True, stop=True)
                ins.then_inc(w["wa"], 1)
                for t in range(2):
                    for h in range(2):
                        pe.matmul(PS[5][hr[h], t * P:(t + 1) * P], TOK[:, t, 3, hr[h]], MR[:, t, h, P:2 * P],
                                  start=True, stop=False)
                    for r in range(2):
                        c = 2 * t + r
                        rr = slice(r * CH, (r + 1) * CH)
                        if c > 0:
                            await_step(w["snew"], 4 * p + c)
                            for h in range(2):
                                ins = pe.matmul(PS[6 - 5 * h][rr, 0:HN], WT[hr[h], t, rr], ST[hr[h], c % 2, :],
                                                start=True, stop=True)
                            ins.then_inc(w["umm"], 1)
                            for h in range(2):
                                pe.matmul(PS[5][hr[h], t * P + r * CH:t * P + (r + 1) * CH], ST[hr[h], c % 2, :],
                                          AR[hr[h], 1, t * P + r * CH:t * P + (r + 1) * CH], start=False, stop=False)
                        await_step(w["uadd"], 4 * p + c + 1)
                        for h in range(2):
                            pe.matmul(PS[7][hr[h], 0:HN], TOK[rr, t, 1, hr[h]], U[rr, t, hr[h]],
                                      start=True, stop=False)
                            ins = pe.matmul(PS[7][hr[h], 0:HN], TOK[rr, t, 2, hr[h]], TOK[rr, t, 3, hr[h]],
                                            start=False, stop=True)
                        ins.then_inc(w["smm"], 1)
                    for h in range(2):
                        pe.matmul(PS[5][hr[h], t * P:(t + 1) * P], U[:, t, hr[h]], LR[:, t, h, P:2 * P],
                                  start=False, stop=True)
                await_step(w["ut"], p + 1)
                for h in range(2):
                    ins = pe.matmul(PS[2][lo32(h), 0:HN], UT[hr[h], :], CP[hr[h], hr[h]], start=True, stop=True)
                ins.then_inc(w["utt"], 1)
                await_step(w["utc"], p + 1)
                for h in range(2):
                    ins = pe.matmul(PS[5][hr[h], SEQ:T], TS[hr[h], 2, :], SM[hr[h], 32:64], start=True, stop=True)
                ins.then_inc(w["ymm"], 1)
                await_step(w["uvx"], p + 1)
                for h in range(2):
                    ins = pe.matmul(PS[0][hr[h], :], TS[hr[h], 1, :], UVX[hr[h], :, :], start=True, stop=True)
                ins.then_inc(w["snmm"], 1)
                await_step(w["snew"], 4 * p + 4)
                pe.transpose(PS[6][0:HN, 256:256 + P], ST[:, 0, :], IDN).then_inc(w["sop"], 1)
                await_step(w["snew2"], p + 1)
                for b in range(4):
                    ins = pe.transpose(PS[1][:, b * P:(b + 1) * P], SNW[:, 2 * b:2 * b + 2, :], IDN)
                ins.then_inc(w["snt"], 1)
                await_step(w["yout"], p + 1)
                pe.matmul(PS[2][:, 0:T], HEADAVG, YR[:, :], start=True, stop=True).then_inc(w["ymean"], 1)
                await_step(w["ysq"], p + 1)
                await_step(w["bonv"], p + 1)
                pe.matmul(PS[3][:, 0:T], HEADAVG, YQ[:, :], start=True, stop=True).then_inc(w["yvar"], 1)

            pe.wait_ge(w["ydone"], KC + 1)
            pe.wait_ge(w["sopc"], KC)
            pe.wait_ge(w["sos"], KC)
            pe.sem_inc(wkv_done, 1)

            for j in range(2):
                take_slab(SLAB["g2"] + j)
            for m in range(KC):
                o = OUT["g2"] + m
                take_bank(o)
                for j in range(2):
                    ins = three(PS[o % 4][:, 0:T], WH[:, j, m * P:(m + 1) * P], WL[:, j, m * P:(m + 1) * P],
                                LHH[:, 2 + j, :], LHL[:, 2 + j, :], j == 0, j == 1)
                ins.then_inc(row_ready, 1)
            pe.drain().then_inc(slab_used, 2)
            pe.wait_ge(ygl_ready, KC)
            square("o", MH[0], ML[0])

            def layer_norm(k):
                pe.wait_ge(ln["x"], k + 1)
                for c in range(KC):
                    ins = pe.matmul(PS[4][:, 0:T], AVG, X[:, c, 1:T + 1], start=c == 0, stop=c == KC - 1)
                ins.then_inc(ln["mean"], 1)
                for q in range(4):
                    pe.wait_ge(ln["sq"], 4 * k + q + 1)
                    for c in range(4 * q, 4 * q + 4):
                        ins = pe.matmul(PS[5][:, 0:T], AVG, SQ[:, c, :], start=c == 0, stop=c == KC - 1)
                ins.then_inc(ln["var"], 1)

            def ffn(layer, lnk):
                pe.wait_ge(ln["lo"], HALVED[lnk] + KC)
                for g in range(2):
                    s0 = SLAB[f"ffn{layer}"] + g * FFN_SLABS
                    o0 = OUT[f"ffn{layer}"] + g * FFN_OUTS
                    pe.wait_ge(out_free, o0 + 4)
                    with pe.Fori(0, HG // 2) as i:
                        for j in range(4):
                            take_slab(s0 + 4 * i + j)
                            take_bank(o0 + 4 * i + j)
                            for k in range(KC):
                                ins = three(PS[j][:, 0:T], WH[:, j % 2, k * P:(k + 1) * P],
                                            WL[:, j % 2, k * P:(k + 1) * P], MH[0][:, k, :], ML[0][:, k, :],
                                            k == 0, k == KC - 1)
                            ins.then_inc(slab_used, 1)
                    s1, o1 = s0 + 2 * HG, o0 + 2 * HG
                    pe.wait_ge(hl_ready, 2 + (2 * layer + g + 1) * HG)
                    with pe.Fori(0, KC // 2) as i:
                        for j in range(4):
                            take_slab(s1 + 4 * i + j)
                            if j % 2 == 0:
                                pe.wait_ge(out_free, o1 + 2 * i + j // 2 + 3)
                            for k in range(HH2):
                                kk = (j % 2) * HH2 + k
                                ins = three(PS[j // 2][:, 0:T], WH[:, j % 2, k * P:(k + 1) * P],
                                            WL[:, j % 2, k * P:(k + 1) * P], HH[:, kk, :], HL[:, kk, :],
                                            kk == 0, kk == HG - 1)
                            ins.then_inc(slab_used, 1)

            layer_norm(0)
            ffn(0, 0)
            pe.wait_ge(past_in, 16)
            for c in range(KC):
                if c % 4 == 0 and c >= 8:
                    pe.wait_ge(pl["past"], c // 4 - 1)
                ins = pe.transpose(PS[6 + c // 4 % 2][:, (c % 4) * P:(c % 4) * P + NSEQ * BUF],
                                   PAST[0:NSEQ * BUF, c * P:(c + 1) * P], CP[0:NSEQ * BUF, 0:NSEQ * BUF])
                if c % 4 == 3:
                    ins.then_inc(pl["pastT"], 1)
            layer_norm(1)
            pe.wait_ge(ln["done"], 2 * KC)
            pe.wait_ge(pl["past"], 4)
            for q in range(4):
                if q >= 2:
                    pe.wait_ge(tr_ready, q - 1)
                for c in range(4):
                    ins = pe.transpose(PS[6 + q % 2][0:48, c * P:(c + 1) * P], X[:, 4 * q + c, T + 1 - 48:T + 1], IDN)
                ins.then_inc(pl["trT"], 1)
            pe.wait_ge(out_free, OUT["pool"] + 4)
            pe.wait_ge(pl["lo"], 1)
            for j in range(4):
                take_slab(SLAB["pool"] + j)
                for m in range(4):
                    o = OUT["pool"] + 4 * j + m
                    take_bank(o)
                    for k in range(4):
                        c = k * 512 + m * P
                        ins = three(PS[m][:, 0:T], WH[:, j % 2, c:c + P], WL[:, j % 2, c:c + P],
                                    MH[0][:, 4 * j + k, :], ML[0][:, 4 * j + k, :], k == 0, k == 3)
                    ins.then_inc(row_ready, 1)
                pe.drain().then_inc(slab_used, 1)
            layer_norm(2)
            ffn(1, 2)
            layer_norm(3)
            pe.wait_ge(ln["done"], 4 * KC)
            for q in range(4):
                for a, n in enumerate((P, P, NS)):
                    z = 3 * q + a
                    if z >= 2:
                        pe.wait_ge(yrow_ready, z - 1)
                    for c in range(4):
                        ins = pe.transpose(PS[6 + z % 2][0:n, c * P:(c + 1) * P],
                                           X[:, 4 * q + c, 1 + a * P:1 + a * P + n], IDN)
                    ins.then_inc(yt["T"], 1)

        @block.scalar
        def _(act):
            def hi(q, j, s, n=2048, rows=P):
                act.wait_ge(raw_landed[j], 16 * (q + 1))
                act.wait_ge(slab_used, s + 1)
                act.activation(WH[0:rows, j % 2, 0:n], RAW[0:rows, j, 0:n], ACT.Copy).then_inc(hi_ready, 1)

            def mix_scale(name, c, b):
                act.wait_ge(mixlo_ready, MIX[name] * KC + c + 1)
                act.activation(TM[:, b, :], X[:, bass.ds(c, 1), 1:T + 1].rearrange("p a t -> p (a t)"), ACT.Copy,
                               scale=OMU[:, bass.ds(MU_ROW[name] * KC + c, 1)]).then_inc(tm_ready, 1)

            def mix_hi(name, c, b):
                q = MIX[name]
                act.wait_ge(mt_ready, q * KC + c + 1)
                act.activation(MH[q % 2][:, bass.ds(c, 1), :].rearrange("p a t -> p (a t)"), TM[:, b, :],
                               ACT.Copy).then_inc(mixhi_ready, 1)

            with act.Fori(0, 4) as i:
                for c in range(4):
                    act.wait_ge(x_turned, 8 + 4 * i + c + 1)
                    act.activation(X[:, bass.ds(4 * i + c, 1), 1:T + 1], PS[c][:, 0:T].rearrange("p (a t) -> p a t", a=1),
                                   ACT.Copy).then_inc(x_ready, 1)
            act.wait_ge(omu_ready, 1)
            act.wait_ge(x_ready, KC)
            widths = (KC * DL, KC * DL, 2048, 2048)
            for name, m in (("w", 0), ("a", 1), ("g", 2)):
                if m == 2:
                    act.wait_ge(slab_used, 2 + 1)
                if m < 2:
                    hi(0, m, m, widths[m])
                mix_scale(name, 0, 0)
                for c in range(KC):
                    if c + 1 < KC:
                        mix_scale(name, c + 1, (c + 1) % 2)
                    mix_hi(name, c, c % 2)

            def low_rank(j, rows, f):
                act.wait_ge(slab_used, 2 + j + 1)
                act.activation(R[0:rows, j, :], PS[j][0:rows, 0:T], f).then_inc(lh_ready, 1)
                act.wait_ge(lh_ready, j + 1)
                act.activation(LHH[0:rows, j, :], R[0:rows, j, :], ACT.Copy).then_inc(lhh_ready, 1)

            low_rank(0, DL, ACT.Tanh)
            hi(0, 2, 2)
            low_rank(1, DL, ACT.Copy)
            hi(0, 3, 3)
            low_rank(2, P, ACT.Sigmoid)
            hi(1, 0, 4)
            low_rank(3, P, ACT.Sigmoid)
            hi(1, 1, 5)
            mix_scale("r", 0, 0)
            for c in range(KC):
                if c + 1 < KC:
                    mix_scale("r", c + 1, (c + 1) % 2)
                mix_hi("r", c, c % 2)
            act.wait_ge(lhl_ready, 4)

            def square(name, evac, extra, n_next, rows_next=P, before=None):
                s0 = SLAB[name]

                def turn(i, last):
                    for j in range(4):
                        s = s0 + 4 * i + j + 2
                        if before is not None:
                            before(4 * i + j, j % 2)
                        if not (last and j >= 2):
                            hi(s0 // 4 + i + (j + 2) // 4, (j + 2) % 4, s)
                        else:
                            hi(s0 // 4 + i + 1, (j + 2) % 4, s, n_next, rows_next)
                        if evac is not None:
                            evac(i, j, s0)
                        if extra is not None:
                            extra(4 * i + j, j % 2)

                with act.Fori(0, 3) as i:
                    turn(i, False)
                turn(3, True)

            def keep(dst):
                def evac(i, j, s0):
                    act.wait_ge(slab_used, s0 + 4 * i + j + 3)
                    ins = act.activation(dst[:, bass.ds(4 * i + j, 1), :].rearrange("p a t -> p (a t)"), PS[j][:, 0:T],
                                         ACT.Copy)
                    ins.then_inc(out_free, 1)
                return evac

            def next_mix(name):
                def extra(c, b):
                    mix_scale(name, c, b)
                    mix_hi(name, c, b)
                return extra

            act.wait_ge(slab_used, 2 + SLAB["r"])
            square("r", keep(R), next_mix("k"), 2048)
            act.wait_ge(slab_used, 2 + SLAB["k"])
            square("k", keep(K), next_mix("v"), 2048)

            def key_squares(c, b):
                act.wait_ge(kk_ready, c + 1)
                act.wait_ge(kc_ready, c + 1)
                act.activation(TM[:, b, :], KK[:, bass.ds(c, 1), :].rearrange("p a t -> p (a t)"), ACT.Square)\
                   .then_inc(kks_ready, 1)

            def key_roots(c, b):
                act.wait_ge(kkn_ready, c + 1)
                act.activation(TM[:, b, :], PS[4 + b][:, 0:T], ACT.Sqrt).then_inc(kkd_ready, 1)

            square("v", keep(V), key_roots, 2048, DL, key_squares)

            for n, (dst, bias) in enumerate(((SG, "w0"), (A, "a0"))):
                with act.Fori(0, 4) as i:
                    for j in range(4):
                        act.wait_ge(row_ready, ROW["lora2"] + n * KC + 4 * i + j + 1)
                        act.activation(dst[:, bass.ds(4 * i + j, 1), :].rearrange("p a t -> p (a t)"), PS[j][:, 0:T],
                                       ACT.Sigmoid, bias=par(bias, 4 * i + j)).then_inc(out_free, 1)

            act.wait_ge(out_free, 4 + OUT["g2"])
            act.wait_ge(wkv_const, 16)
            link = Chain(act, w["aself"], 1)
            hr = [slice(0, HN), slice(HN, P)]
            with act.Fori(0, KC) as p:
                link.turn(p)
                act.wait_ge(w["ydone"], p + 1)
                act.wait_ge(w["s0free"], p + 1)
                act.wait_ge(w["cs"], 2 * p + 1)
                act.activation(PC[:, :], CS[:, :], ACT.Exp, scale=DECAY)
                act.activation(IPC[:, :], CS[:, :], ACT.Exp, scale=-DECAY)
                act.wait_ge(w["cs"], 2 * p + 2)
                act.activation(PPC[:, :], CSX[:, :], ACT.Exp, scale=DECAY).then_inc(w["decays"], 1)
                act.activation(VF[:, :], V[:, bass.ds(p, 1), :].rearrange("p a t -> p (a t)"), ACT.Copy)\
                   .then_inc(w["vcopy"], 1)
                act.wait_ge(w["s0t"], p + 2)
                act.activation(S0T[:, :, :].rearrange("p b v -> p (b v)"), PS[0][:, :], ACT.Copy).then_inc(w["s0c"], 1)
                act.wait_ge(w["tokT"], p + 1)
                for t in range(2):
                    act.activation(TOK[:, t, :, :].rearrange("p n f -> p (n f)"), PS[1 + t][:, :], ACT.Copy)
                act.activation(TS[:, :, :].rearrange("p n f -> p (n f)"), PS[3][:, 0:3 * HN], ACT.Copy)\
                   .then_inc(w["tok"], 1)
                act.wait_ge(w["t2"], p + 1)
                act.activation(TI[:, :, :].rearrange("p u t -> p (u t)"), PS[1][:, :], ACT.Copy)
                for h in range(2):
                    ins = act.activation(STI[h * HN:h * HN + 32, :], PS[2][h * HN:h * HN + 32, 0:NS], ACT.Copy)
                ins.then_inc(w["t2c"], 1)
                for lv in range(4):
                    act.wait_ge(w["ttt"], 4 * p + lv + 1)
                    act.activation(TIT[:, :, :].rearrange("p u t -> p (u t)"), PS[6][:, :], ACT.Copy)\
                       .then_inc(w["ttc"], 1)
                act.wait_ge(w["mv"], p + 1)
                act.activation(MV[:, :, :].rearrange("p u v -> p (u v)"), PS[7][:, 0:256], ACT.Copy)
                for h in range(2):
                    ins = act.activation(MVS[h * HN:h * HN + 32, :], PS[7][h * HN:h * HN + 32, 256:256 + HN], ACT.Copy)
                ins.then_inc(w["mvc"], 1)
                act.wait_ge(w["q"], p + 1)
                act.activation(WT[:, :, :].rearrange("p t s -> p (t s)"), PS[1][:, 0:256], ACT.Copy)
                act.activation(WR[:, :, 0:4], PS[1][:, 256:256 + NS].rearrange("p (b t) -> p b t", b=NSEQ), ACT.Copy)
                act.activation(WR[:, :, 4:8], AR[:, 1, SEQ:T].rearrange("p (b t) -> p b t", b=NSEQ), ACT.Copy)
                act.activation(QT[:, :], PS[1][:, 320:320 + NS], ACT.Copy)
                act.activation(Q[:, :, :].rearrange("p u v -> p (u v)"), PS[2][:, 0:256], ACT.Copy).then_inc(w["qc"], 1)
                act.wait_ge(w["sop"], p + 1)
                act.activation(SOP[:, :], PS[6][0:HN, 256:256 + P], ACT.Copy).then_inc(w["sopc"], 1)
                act.wait_ge(w["snt"], p + 1)
                act.activation(SOS[:, :, :].rearrange("p b k -> p (b k)"), PS[1][:, :], ACT.Copy).then_inc(w["sos"], 1)
                act.wait_ge(w["ycen"], p + 1)
                act.activation(YQ[:, :], YC[:, :], ACT.Square).then_inc(w["ysq"], 1)
                act.wait_ge(w["yvar"], p + 1)
                link(act.activation(YD[:, :], PS[3][:, 0:T], ACT.Copy, bias=GN_EPS))
                act.activation(YD[:, :], YD[:, :], ACT.Sqrt).then_inc(w["ysd"], 1)
            act.wait_ge(w["ydone"], KC + 1)
            act.wait_ge(wkv_done, 3)

            hi(13, 2, SLAB["g2"])
            hi(13, 3, SLAB["g2"] + 1)
            with act.Fori(0, KC) as c:
                act.wait_ge(yg_ready, c + 1)
                act.activation(MH[0][:, bass.ds(c, 1), :].rearrange("p a t -> p (a t)"),
                               R[:, bass.ds(c, 1), :].rearrange("p a t -> p (a t)"), ACT.Copy).then_inc(ygh_ready, 1)
            hi(14, 0, SLAB["o"])
            hi(14, 1, SLAB["o"] + 1)
            square("o", None, None, 2048)

            def layer_norm(k, halves):
                for q in range(4):
                    act.wait_ge(ln["cen"], 4 * k + q + 1)
                    act.activation(SQ[:, 4 * q:4 * q + 4, :], X[:, 4 * q:4 * q + 4, 1:T + 1], ACT.Square)\
                       .then_inc(ln["sq"], 1)
                act.wait_ge(ln["var"], k + 1)
                act.activation(LNS[:, 0, :], PS[5][:, 0:T], ACT.Copy, bias=LN_EPS).then_inc(ln["sd"], 1)
                act.wait_ge(ln["sd"], 2 * k + 1)
                act.activation(LNS[:, 0, :], LNS[:, 0, :], ACT.Sqrt).then_inc(ln["sd"], 1)
                with act.Fori(0, KC) as c:
                    act.wait_ge(ln["scaled"], k * KC + c + 1)
                    xc = X[:, bass.ds(c, 1), 1:T + 1].rearrange("p a t -> p (a t)")
                    act.activation(xc, xc, ACT.Identity, bias=par("ln_b", k * KC + c)).then_inc(ln["done"], 1)
                    if halves:
                        act.wait_ge(ln["done"], k * KC + c + 1)
                        act.activation(MH[0][:, bass.ds(c, 1), :].rearrange("p a t -> p (a t)"), xc, ACT.Copy)\
                           .then_inc(ln["hi"], 1)

            def ffn(layer, n_after):
                for g in range(2):
                    s0 = SLAB[f"ffn{layer}"] + g * FFN_SLABS
                    o0 = OUT[f"ffn{layer}"] + g * FFN_OUTS

                    def up(i, last):
                        for j in range(4):
                            hi(s0 // 4 + i + (j + 2) // 4, (j + 2) % 4, s0 + 4 * i + j + 2,
                               HH2 * P if last and j >= 2 else 2048)
                            if j % 2:
                                b = j // 2
                                hc = 2 * i + b
                                n = (2 * layer + g) * HG + hc
                                act.wait_ge(slab_used, s0 + 4 * i + j + 3)
                                act.wait_ge(hl_ready, n + 1)
                                act.activation(TM[:, b, :], PS[j - 1][:, 0:T], ACT.Sigmoid).then_inc(sg_ready, 1)
                                act.wait_ge(hid_ready, n + 1)
                                act.activation(HH[:, bass.ds(hc, 1), :].rearrange("p a t -> p (a t)"), TM[:, b, :],
                                               ACT.Copy).then_inc(hh_ready, 1)

                    with act.Fori(0, HG // 2 - 1) as i:
                        up(i, False)
                    up(HG // 2 - 1, True)
                    s1 = s0 + 2 * HG
                    with act.Fori(0, KC // 2 - 1) as i:
                        for j in range(4):
                            hi(s1 // 4 + i + (j + 2) // 4, (j + 2) % 4, s1 + 4 * i + j + 2, HH2 * P)
                    for j in range(4):
                        i = KC // 2 - 1
                        if j >= 2 and g == 1 and n_after == 0:
                            continue
                        hi(s1 // 4 + i + (j + 2) // 4, (j + 2) % 4, s1 + 4 * i + j + 2, HH2 * P if j < 2 else 2048)

            layer_norm(0, True)
            ffn(0, 2048)
            for q in range(4):
                act.wait_ge(pl["pastT"], q + 1)
                for c in range(4 * q, 4 * q + 4):
                    ins = act.activation(ES[0][:, c, :, 0:BUF],
                                         PS[6 + q % 2][:, (c % 4) * P:(c % 4) * P + NSEQ * BUF]
                                         .rearrange("p (b t) -> p b t", b=NSEQ), ACT.Copy)
                ins.then_inc(pl["past"], 1)
            layer_norm(1, False)
            for q in range(4):
                act.wait_ge(pl["trT"], q + 1)
                act.activation(TR[:, q * 512:(q + 1) * 512], PS[6 + q % 2][0:48, :], ACT.Copy).then_inc(tr_ready, 1)
            act.wait_ge(pl["d"], 1)
            act.wait_ge(tr_ready, 5)
            act.activation(MH[0][:, :, :], DP[:, :, :], ACT.Copy).then_inc(pl["hi"], 1)
            for j in range(4):
                q = SLAB["pool"] // 4 + (j + 2) // 4
                hi(q, (j + 2) % 4, SLAB["pool"] + j + 2)
                for m in range(4):
                    n = 4 * j + m
                    act.wait_ge(row_ready, ROW["pool"] + n + 1)
                    act.wait_ge(pl["scaled"], n + 1)
                    act.activation(TM[:, n % 2, :], PS[m][:, 0:T], ACT.Copy, scale=PAR[:, PCOL["scale"] + n:PCOL["scale"] + n + 1])\
                       .then_inc(out_free, 1)
            layer_norm(2, True)
            ffn(1, 0)
            layer_norm(3, False)
            for q in range(4):
                for a, n in enumerate((P, P, NS)):
                    z = 3 * q + a
                    act.wait_ge(yt["T"], z + 1)
                    act.activation(YROW[0:n, a, q * 512:(q + 1) * 512], PS[6 + z % 2][0:n, :], ACT.Copy)\
                       .then_inc(yrow_ready, 1)

        @block.vector
        def _(dve):
            def lo(s, j, n=2048, rows=P):
                dve.wait_ge(hi_ready, s + 1)
                dve.tensor_tensor(WL[0:rows, j % 2, 0:n], RAW[0:rows, j, 0:n], WH[0:rows, j % 2, 0:n].bitcast(F32),
                                  ALU.subtract).then_inc(lo_ready, 1)

            def one(t, c):
                return t[:, bass.ds(c, 1), :].rearrange("p a t -> p (a t)")

            def mix_add(name, c, b):
                mu = PAR[:, bass.ds(MU_ROW[name] * KC + c, 1)]
                dve.wait_ge(tm_ready, MIX[name] * KC + c + 1)
                dve.scalar_tensor_tensor(out=TM[:, b, 0:SEQ],
                                         in0=X[:, bass.ds(c, 1), 0:SEQ].rearrange("p a t -> p (a t)"), scalar=mu,
                                         in1=TM[:, b, 0:SEQ], op0=ALU.mult, op1=ALU.add)
                dve.scalar_tensor_tensor(out=TM[:, b, SEQ:T], in0=one(XPS, c), scalar=mu, in1=TM[:, b, SEQ:T],
                                         op0=ALU.mult, op1=ALU.add).then_inc(mt_ready, 1)

            def mix_lo(name, c, b):
                q = MIX[name]
                dve.wait_ge(mixhi_ready, q * KC + c + 1)
                dve.tensor_tensor(one(ML[q % 2], c), TM[:, b, :], one(MH[q % 2], c).bitcast(F32), ALU.subtract)\
                   .then_inc(mixlo_ready, 1)

            dve.wait_ge(par_turned, 1)
            dve.tensor_copy(PAR[:, 0:P + 96], PS[4][:, 0:P + 96])
            dve.tensor_copy(PAR[:, 256:384], PS[4][:, 256:384]).then_inc(par_ready, 1)
            dve.wait_ge(par_ready, 1)
            dve.tensor_scalar(OMU[:, :], PAR[:, 0:96], -1.0, 1.0, ALU.mult, ALU.add).then_inc(omu_ready, 1)
            dve.memset(X[:, :, 0:1], 0.0)
            with dve.Fori(0, 4) as i:
                for c in range(4):
                    dve.wait_ge(x_ready, 4 * i + c + 1)
                    dst = one(XPS, 4 * i + c).rearrange("p (b t) -> p b t", b=NSEQ)
                    dve.tensor_copy(dst[:, :, 0:1], PS[c][:, T:T + NSEQ].rearrange("p (b t) -> p b t", t=1))
                    dve.tensor_copy(dst[:, :, 1:NSTEP],
                                    PS[c][:, SEQ:T].rearrange("p (b t) -> p b t", b=NSEQ)[:, :, 0:NSTEP - 1])\
                       .then_inc(x_bank_free, 1)
            dve.wait_ge(x_bank_free, 4 + KC)
            widths = (KC * DL, KC * DL, 2048, 2048)
            for name, m in (("w", 0), ("a", 1), ("g", 2)):
                if m < 2:
                    lo(m, m, widths[m])
                mix_add(name, 0, 0)
                for c in range(KC):
                    if c + 1 < KC:
                        mix_add(name, c + 1, (c + 1) % 2)
                    mix_lo(name, c, c % 2)

            def low_rank(j, rows):
                dve.wait_ge(lhh_ready, j + 1)
                dve.tensor_tensor(LHL[0:rows, j, :], R[0:rows, j, :], LHH[0:rows, j, :].bitcast(F32), ALU.subtract)\
                   .then_inc(lhl_ready, 1)
                dve.sem_inc(out_free, 1)

            low_rank(0, DL)
            lo(2, 2)
            low_rank(1, DL)
            lo(3, 3)
            low_rank(2, P)
            lo(4, 0)
            low_rank(3, P)
            lo(5, 1)
            mix_add("r", 0, 0)
            for c in range(KC):
                if c + 1 < KC:
                    mix_add("r", c + 1, (c + 1) % 2)
                mix_lo("r", c, c % 2)

            def square(name, evac, extra, n_next, rows_next=P, before=None):
                s0 = SLAB[name]

                def turn(i, last):
                    for j in range(4):
                        s = s0 + 4 * i + j + 2
                        if before is not None:
                            before(4 * i + j, j % 2)
                        if not (last and j >= 2):
                            lo(s, (j + 2) % 4)
                        else:
                            lo(s, (j + 2) % 4, n_next, rows_next)
                        if evac is not None:
                            evac(i, j, s0)
                        if extra is not None:
                            extra(4 * i + j, j % 2)

                with dve.Fori(0, 3) as i:
                    turn(i, False)
                turn(3, True)

            def next_mix(name):
                def extra(c, b):
                    mix_add(name, c, b)
                    mix_lo(name, c, b)
                return extra

            square("r", None, next_mix("k"), 2048)
            square("k", None, next_mix("v"), 2048)
            link = Chain(dve, kk_self, 2)

            def keys(c, b):
                dve.tensor_scalar(one(KK, c), one(K, c), par("k_k", c), None, ALU.mult).then_inc(kc_ready, 1)

            def unit_keys(c, b):
                link.turn(c)
                dve.wait_ge(kkd_ready, c + 1)
                link(dve.tensor_scalar(TM[:, b, :], TM[:, b, :], 1e-12, None, ALU.max))
                link(dve.reciprocal(TM[:, b, :], TM[:, b, :]))
                dve.tensor_tensor(one(KK, c), one(KK, c), TM[:, b, :], ALU.mult).then_inc(kk_ready, 1)

            dve.wait_ge(out_free, 4 + OUT["v"])
            square("v", None, unit_keys, 2048, DL, keys)
            dve.wait_ge(out_free, 4 + OUT["g2"])
            dve.wait_ge(kk_ready, 2 + KC)
            dve.wait_ge(lo_ready, 4 + SLAB["g2"])
            dve.sem_inc(wkv_go, 1)

            dve.wait_ge(wkv_const, 16)
            dve.sem_inc(w["ydone"], 1)
            dve.sem_inc(w["s0free"], 1)
            link = Chain(dve, w["self"], 11)
            hr = [slice(0, HN), slice(HN, P)]
            with dve.Fori(0, KC) as p:
                link.turn(p)
                sg = one(SG, p)
                dve.tensor_tensor_scan(CS[:, :], NOTSTART, sg, 0.0, ALU.mult, ALU.add).then_inc(w["cs"], 1)
                dve.wait_ge(w["cs"], 2 * p + 1)
                dve.tensor_tensor(CSX[:, :], CS[:, :], sg, ALU.subtract).then_inc(w["cs"], 1)
                link(dve.tensor_scalar(KT[:, :], one(A, p), -1.0, par("k_a", p), ALU.add, ALU.mult))
                link(dve.scalar_tensor_tensor(out=KT[:, :], in0=KT[:, :], scalar=1.0, in1=one(K, p), op0=ALU.add,
                                              op1=ALU.mult))
                link(dve.tensor_tensor(BF[:, :], one(KK, p), one(A, p), ALU.mult))
                dve.scalar_tensor_tensor(out=RKP[:, :], in0=one(R, p), scalar=par("r_k", p), in1=KT[:, :],
                                         op0=ALU.mult, op1=ALU.mult).then_inc(w["rkp"], 1)
                dve.wait_ge(w["decays"], p + 1)
                dve.scalar_tensor_tensor(out=AR[:, 0, :], in0=one(KK, p), scalar=-1.0, in1=PPC[:, :], op0=ALU.mult,
                                         op1=ALU.mult)
                dve.tensor_tensor(AR[:, 1, :], one(R, p), PC[:, :], ALU.mult)
                dve.tensor_tensor(BF[:, :], BF[:, :], IPC[:, :], ALU.mult)
                dve.tensor_tensor(KF[:, :], KT[:, :], IPC[:, :], ALU.mult).then_inc(w["feats"], 1)
                dve.wait_ge(w["prod"], p + 1)
                for h in range(2):
                    for dst, bank in ((LR, 4), (MR, 6)):
                        dve.tensor_tensor(dst[:, :, h, :], PS[bank + h][:, :].rearrange("p (t n) -> p t n", t=2),
                                          M_PROD.unsqueeze(1).broadcast_to([P, 2, 256]), ALU.mult)
                link(dve.tensor_tensor(SM[:, :], PS[0][:, 0:64], MS_PROD, ALU.mult))
                link(dve.tensor_tensor(TIT[:, :, :], LR[:, :, :, 0:P].rearrange("p t h s -> p (t h) s"),
                                       M_ONE.unsqueeze(1).broadcast_to([P, 4, P]), ALU.mult))
                link(dve.tensor_tensor(STT[:, :], SM[:, 0:NS], MS_ONE, ALU.mult))
                dve.tensor_tensor(TIT[:, :, :], TIT[:, :, :], IDN.unsqueeze(1).broadcast_to([P, 4, P]), ALU.add)
                dve.tensor_tensor(STT[:, :], STT[:, :], IDS, ALU.add).then_inc(w["t2t"], 1)
                for lv in range(5):
                    dve.wait_ge(w["xmm"], 5 * p + lv + 1)
                    if lv == 0:
                        for h in range(2):
                            q = slice(h * HN, h * HN + 32)
                            dve.tensor_tensor(SXL[q, :], PS[4][q, 0:NS], MS_TWO[q, :], ALU.mult)
                    dve.tensor_tensor(XL[:, :, :], PS[3][:, :].rearrange("p (u t) -> p u t", u=4),
                                      M_LEVEL[lv].unsqueeze(1).broadcast_to([P, 4, P]), ALU.mult).then_inc(w["xmask"], 1)
                    dve.wait_ge(w["tmm"], 5 * p + lv + 1)
                    if lv == 0:
                        for h in range(2):
                            q = slice(h * HN, h * HN + 32)
                            dve.tensor_tensor(STT[q, :], PS[4][q, 64:64 + NS], STT[q, :], ALU.add)
                    dst = TI if lv < 4 else TIT
                    dve.tensor_tensor(dst[:, :, :], PS[5][:, :].rearrange("p (u t) -> p u t", u=4), dst[:, :, :],
                                      ALU.add).then_inc(w["tadd"], 1)
                dve.wait_ge(w["bon"], p + 1)
                dve.tensor_tensor(RKP[:, :], PS[3][:, 0:T], one(V, p), ALU.mult).then_inc(w["bonv"], 1)
                dve.wait_ge(w["wa"], p + 1)
                was = PS[4][:, 0:64].rearrange("p (b n) -> p b n", b=NSEQ)
                dve.tensor_tensor(UT[:, :].rearrange("p (b t) -> p b t", b=NSEQ), was[:, :, 0:4],
                                  QT[:, :].rearrange("p (b t) -> p b t", b=NSEQ), ALU.add).then_inc(w["ut"], 1)
                for c in range(4):
                    t, r = c // 2, c % 2
                    rr = slice(r * CH, (r + 1) * CH)
                    last = t * P + (r + 1) * CH - 1
                    if c == 0:
                        dve.tensor_copy(U[rr, t, :], Q[rr, 0:2, :].rearrange("p h v -> p (h v)")).then_inc(w["uadd"], 1)
                    else:
                        dve.tensor_scalar(SPD[:, :], ST[:, c % 2, :], PC[:, last:last + 1], None, ALU.mult)\
                           .then_inc(w["spd"], 1)
                        dve.wait_ge(w["umm"], 3 * p + c)
                        for h in range(2):
                            ins = dve.tensor_tensor(U[rr, t, hr[h]], PS[6 - 5 * h][rr, 0:HN], Q[rr, 2 * t + h, :], ALU.add)
                        ins.then_inc(w["uadd"], 1)
                    dve.wait_ge(w["smm"], 4 * p + c + 1)
                    if c == 0:
                        ins = dve.tensor_scalar(ST[:, 1, :], PS[7][:, 0:HN], PC[:, last:last + 1], None, ALU.mult)
                    else:
                        dve.wait_ge(w["spd"], 3 * p + c)
                        ins = dve.scalar_tensor_tensor(out=ST[:, (c + 1) % 2, :], in0=PS[7][:, 0:HN],
                                                       scalar=PC[:, last:last + 1], in1=SPD[:, :], op0=ALU.mult,
                                                       op1=ALU.add)
                    ins.then_inc(w["snew"], 1)
                    if c < 3:
                        dve.wait_ge(w["snew"], 4 * p + c + 1)
                dve.wait_ge(w["utt"], p + 1)
                for h in range(2):
                    q = slice(h * HN, h * HN + 32)
                    ins = dve.tensor_copy(TS[q, 2, :], PS[2][q, 0:HN])
                ins.then_inc(w["utc"], 1)
                dve.wait_ge(w["utc"], p + 1)
                dve.tensor_tensor(UVX[:, :, :], TS[:, 2, :].unsqueeze(1).broadcast_to([P, NSEQ, HN]),
                                  MS_SEQ.unsqueeze(2).broadcast_to([P, NSEQ, HN]), ALU.mult).then_inc(w["uvx"], 1)
                dve.wait_ge(w["ymm"], p + 1)
                dve.tensor_copy(YR[:, 0:SEQ], PS[5][:, 0:SEQ])
                link(dve.tensor_copy(YR[:, SEQ:T].rearrange("p (b t) -> p b t", b=NSEQ), was[:, :, 4:8]))
                dve.tensor_tensor(YR[:, SEQ:T], PS[5][:, SEQ:T], YR[:, SEQ:T], ALU.add).then_inc(w["yout"], 1)
                dve.wait_ge(w["snmm"], p + 1)
                link(dve.tensor_tensor(SNW[:, :, :], PS[0][:, :].rearrange("p (b v) -> p b v", b=NSEQ), S0T[:, :, :],
                                       ALU.add))
                ends = PC[:, SEQ:T].rearrange("p (b t) -> p b t", b=NSEQ)[:, :, NSTEP - 1:NSTEP]
                dve.tensor_tensor(SNW[:, :, :], SNW[:, :, :], ends.broadcast_to([P, NSEQ, HN]), ALU.mult)\
                   .then_inc(w["snew2"], 1)
                dve.wait_ge(w["ymean"], p + 1)
                dve.tensor_tensor(YC[:, :], YR[:, :], PS[2][:, 0:T], ALU.subtract).then_inc(w["ycen"], 1)
                dve.wait_ge(w["ysd"], p + 1)
                link(dve.reciprocal(YD[:, :], YD[:, :]))
                link(dve.tensor_tensor(YC[:, :], YC[:, :], YD[:, :], ALU.mult))
                link(dve.tensor_scalar(YC[:, :], YC[:, :], par("gn_g", p), par("gn_b", p), ALU.mult, ALU.add))
                dve.tensor_tensor(one(R, p), YC[:, :], RKP[:, :], ALU.add).then_inc(w["ydone"], 1)
                assert link.n == link.per, link.n
            dve.wait_ge(w["ydone"], KC + 1)
            dve.sem_inc(wkv_done, 1)

            lo(SLAB["g2"], 2)
            lo(SLAB["g2"] + 1, 3)
            with dve.Fori(0, 4) as i:
                for j in range(4):
                    c = 4 * i + j
                    dve.wait_ge(row_ready, ROW["g2"] + c + 1)
                    dve.tensor_tensor(one(R, c), PS[j][:, 0:T], one(R, c), ALU.mult).then_inc(yg_ready, 1)
                    dve.wait_ge(ygh_ready, c + 1)
                    dve.sem_inc(out_free, 1)
                    dve.tensor_tensor(one(ML[0], c), one(R, c), one(MH[0], c).bitcast(F32), ALU.subtract)\
                       .then_inc(ygl_ready, 1)
            lo(SLAB["o"], 0)
            lo(SLAB["o"] + 1, 1)

            def xcur(c):
                return X[:, bass.ds(c, 1), 1:T + 1].rearrange("p a t -> p (a t)")

            def residual(i, j, s0):
                dve.wait_ge(slab_used, s0 + 4 * i + j + 3)
                dve.scalar_tensor_tensor(out=xcur(4 * i + j), in0=xcur(4 * i + j), scalar=ALPHA, in1=PS[j][:, 0:T],
                                         op0=ALU.mult, op1=ALU.add).then_inc(out_free, 1)

            square("o", residual, None, 2048)

            def layer_norm(k, halves, freed):
                dve.wait_ge(out_free, 4 + freed)
                dve.sem_inc(ln["x"], 1)
                dve.wait_ge(ln["mean"], k + 1)
                for q in range(4):
                    xs = X[:, 4 * q:4 * q + 4, 1:T + 1]
                    dve.tensor_tensor(xs, xs, PS[4][:, 0:T].unsqueeze(1).broadcast_to([P, 4, T]), ALU.subtract)\
                       .then_inc(ln["cen"], 1)
                dve.wait_ge(ln["sd"], 2 * k + 2)
                dve.reciprocal(LNS[:, 1, :], LNS[:, 0, :]).then_inc(ln["rstd"], 1)
                dve.wait_ge(ln["rstd"], k + 1)
                dve.wait_ge(ln["cen"], 4 * k + 4)
                with dve.Fori(0, KC) as c:
                    dve.scalar_tensor_tensor(out=xcur(c), in0=xcur(c), scalar=par("ln_g", k * KC + c),
                                             in1=LNS[:, 1, :], op0=ALU.mult, op1=ALU.mult).then_inc(ln["scaled"], 1)
                    if halves:
                        dve.wait_ge(ln["hi"], HALVED[k] + c + 1)
                        dve.tensor_tensor(one(ML[0], c), xcur(c), one(MH[0], c).bitcast(F32), ALU.subtract)\
                           .then_inc(ln["lo"], 1)

            def ffn(layer, n_after):
                for g in range(2):
                    s0 = SLAB[f"ffn{layer}"] + g * FFN_SLABS
                    o0 = OUT[f"ffn{layer}"] + g * FFN_OUTS

                    def up(i, last):
                        for j in range(4):
                            lo(s0 + 4 * i + j + 2, (j + 2) % 4, HH2 * P if last and j >= 2 else 2048)
                            if j % 2:
                                b = j // 2
                                hc = 2 * i + b
                                n = (2 * layer + g) * HG + hc
                                dve.wait_ge(sg_ready, n + 1)
                                dve.tensor_tensor(TM[:, b, :], TM[:, b, :], PS[j - 1][:, 0:T], ALU.mult)\
                                   .then_inc(hid_self, 1)
                                dve.wait_ge(hid_self, n + 1)
                                dve.tensor_tensor(TM[:, b, :], TM[:, b, :], PS[j][:, 0:T], ALU.mult)\
                                   .then_inc(hid_ready, 1)
                                dve.wait_ge(hid_ready, n + 1)
                                dve.sem_inc(out_free, 2)
                                dve.wait_ge(hh_ready, n + 1)
                                dve.tensor_tensor(one(HL, hc), TM[:, b, :], one(HH, hc).bitcast(F32), ALU.subtract)\
                                   .then_inc(hl_ready, 1)

                    with dve.Fori(0, HG // 2 - 1) as i:
                        up(i, False)
                    up(HG // 2 - 1, True)
                    s1, o1 = s0 + 2 * HG, o0 + 2 * HG

                    def down(i, j):
                        c = 2 * i + j // 2
                        dve.wait_ge(slab_used, s1 + 4 * i + j + 3)
                        if g == 0:
                            ins = dve.scalar_tensor_tensor(out=xcur(c), in0=xcur(c), scalar=ALPHA,
                                                           in1=PS[j // 2][:, 0:T], op0=ALU.mult, op1=ALU.add)
                        else:
                            ins = dve.tensor_tensor(xcur(c), xcur(c), PS[j // 2][:, 0:T], ALU.add)
                        ins.then_inc(out_free, 1)

                    with dve.Fori(0, KC // 2 - 1) as i:
                        for j in range(4):
                            lo(s1 + 4 * i + j + 2, (j + 2) % 4, HH2 * P)
                            if j % 2:
                                down(i, j)
                    for j in range(4):
                        i = KC // 2 - 1
                        if not (j >= 2 and g == 1 and n_after == 0):
                            lo(s1 + 4 * i + j + 2, (j + 2) % 4, HH2 * P if j < 2 else 2048)
                        if j % 2:
                            down(i, j)

            layer_norm(0, True, OUT["ffn0"])
            ffn(0, 2048)
            dve.wait_ge(out_free, 4 + OUT["pool"])
            dve.sem_inc(past_go, 2)
            layer_norm(1, False, OUT["pool"])
            dve.wait_ge(ln["done"], 2 * KC)
            link = Chain(dve, pl["self"])
            dve.memset(EP[0][:, :, 0:BUF], 0.0)
            dve.tensor_copy(EP[0][:, :, BUF:], X[:, :, 1:SEQ + 1])
            dve.wait_ge(pl["past"], 4)
            with dve.Fori(0, KC) as c:
                ins = dve.tensor_copy(ES[0][:, bass.ds(c, 1), :, BUF:].rearrange("p a b t -> p (a b) t"),
                                      X[:, bass.ds(c, 1), SEQ + 1:T + 1].rearrange("p a (b t) -> p (a b) t", b=NSEQ))
                ins.then_inc(pl["ext"], 1)
            dve.wait_ge(pl["ext"], KC)
            for lv in range(4):
                d, f = 1 << lv, 4 * lv
                a, b = lv % 2, (lv + 1) % 2
                m = (2 << lv) - 1
                n = KC - f
                link(dve.tensor_tensor(EP[b][:, f:KC, m:], EP[a][:, f:KC, m:], EP[a][:, f:KC, m - d:BUF + SEQ - d],
                                       ALU.add))
                es = [e[:, f:KC, :, :].rearrange("p c b t -> p (c b) t") for e in ES]
                link(dve.tensor_tensor(es[b][:, :, m:], es[a][:, :, m:], es[a][:, :, m - d:BUF + NSTEP - d], ALU.add))
                win = 2 << lv
                gs = slice(4 * lv, 4 * lv + 4)
                dve.wait_ge(inv_in, 16)
                link(dve.tensor_tensor(EP[b][:, gs, BUF:BUF + 16], EP[b][:, gs, BUF:BUF + 16],
                                       CI[:, lv, :].unsqueeze(1).broadcast_to([P, 4, 16]), ALU.mult))
                dve.scalar_tensor_tensor(out=DP[:, gs, 0:SEQ], in0=EP[b][:, gs, BUF:], scalar=1.0 / win,
                                         in1=X[:, gs, 1:SEQ + 1], op0=ALU.mult, op1=ALU.subtract)
                for c in range(4 * lv, 4 * lv + 4):
                    ins = dve.scalar_tensor_tensor(
                        out=DP[:, c, SEQ:T].rearrange("p (b t) -> p b t", b=NSEQ), in0=ES[b][:, c, :, BUF:],
                        scalar=1.0 / win, in1=X[:, c, SEQ + 1:T + 1].rearrange("p (b t) -> p b t", b=NSEQ),
                        op0=ALU.mult, op1=ALU.subtract)
            ins.then_inc(pl["d"], 1)
            dve.wait_ge(pl["hi"], 1)
            dve.tensor_tensor(ML[0][:, :, :], DP[:, :, :], MH[0][:, :, :].bitcast(F32), ALU.subtract)\
               .then_inc(pl["lo"], 1)
            dve.sem_inc(pl["scaled"], 2)
            for j in range(4):
                lo(SLAB["pool"] + j + 2, (j + 2) % 4)
                for m in range(4):
                    n = 4 * j + m
                    dve.wait_ge(out_free, 4 + OUT["pool"] + n + 1)
                    dve.scalar_tensor_tensor(out=X[:, n, 1:T + 1], in0=X[:, n, 1:T + 1], scalar=ALPHA,
                                             in1=TM[:, n % 2, :], op0=ALU.mult, op1=ALU.add).then_inc(pl["scaled"], 1)
            dve.wait_ge(pl["scaled"], 2 + KC)
            layer_norm(2, True, OUT["ffn1"])
            ffn(1, 0)
            layer_norm(3, False, OUT["ffn1"] + 2 * FFN_OUTS)


_INS = ["x_prompt", "x_sample", "state_wkv", "state_shift", "state_pool", "ln_g", "ln_b", "rw_mu", "rw_wr", "rw_wk",
        "rw_wv", "rw_wo", "rw_w0", "rw_w1", "rw_w2", "rw_a0", "rw_a1", "rw_a2", "rw_g1", "rw_g2", "rw_kk", "rw_ka",
        "rw_rk", "rw_gn_g", "rw_gn_b", "pool_w", "pool_scale", "ffn_w_in", "ffn_w_down"]
_OUTS = [(1, SEQ, D), (NSEQ, NSTEP, D), (1, 1, H, HN, HN), (1, 1, D), (1, 1, BUF, D), (1, NSEQ, H, HN, HN),
         (1, NSEQ, D), (1, NSEQ, BUF, D)]


def kernel(**inputs):
    import concourse.bacc as _bacc
    from concourse import mybir as _mybir
    from concourse.bass_utils import run_bass_kernel_spmd as _run

    nc = _bacc.Bacc("TRN2", target_bir_lowering=False, num_devices=1)
    arrays, args = {}, []
    given = [(n, np.ascontiguousarray(inputs[n])) for n in _INS]
    given += list(zip(("c_perm", "c_wkv", "c_inv"), shape_constants()))
    for name, a in given:
        arrays[f"in_{name}"] = a
        args.append(nc.dram_tensor(f"in_{name}", a.shape, _mybir.dt.from_np(a.dtype), kind="ExternalInput").ap())
    for i, shape in enumerate(_OUTS):
        args.append(nc.dram_tensor(f"out_{i}", shape, F32, kind="ExternalOutput").ap())
    build(nc, *args)
    r = _run(nc, [arrays], core_ids=[0])
    return tuple(r.results[0][f"out_{i}"] for i in range(len(_OUTS)))
```

```python
from contextlib import ExitStack

import numpy as np

import concourse.bass as bass
from concourse import mybir

F32 = mybir.dt.float32
F32R = mybir.dt.float32r
ACT = mybir.ActivationFunctionType
ALU = mybir.AluOpType

D = 2048
SEQ = 256
NSEQ, NSTEP = 8, 4
NS = NSEQ * NSTEP
T = SEQ + NS
HN = 64
H = D // HN
FF = 5632
P = 128
KC = D // P
FC = FF // P
HG = FC // 2
HH2 = HG // 2
DL = 96
GL = 256
BUF = 15
ALPHA = 4.0 ** 0.25
LN_EPS = 1e-5
GN_EPS = 64e-5
DECAY = -float(np.exp(-0.5))
CH = 64

SLAB = dict(lora1=0, r=4, k=20, v=36, lora2=52, g2=54, o=56, ffn0=72, pool=224, ffn1=228)
OUT = dict(lora1=0, r=4, k=20, v=36, lora2=52, g2=84, o=100, ffn0=116, pool=236, ffn1=252)
ROW = dict(lora2=0, g2=32, pool=48)
FFN_SLABS, FFN_OUTS = 76, 60
MIX = dict(w=0, a=1, g=2, r=3, k=4, v=5)
MU_ROW = dict(r=0, w=1, k=2, v=3, a=4, g=5)

PCOL = dict(w0=96, a0=112, k_k=128, k_a=144, r_k=160, gn_g=176, gn_b=192, scale=208, ln_g=256, ln_b=320)


def shape_constants():
    i = np.arange(P)[:, None]
    j = np.arange(P)[None, :]
    same = (i // CH) == (j // CH)
    cols = [np.eye(P), np.full((P, P), 1.0 / D), same, same / HN]
    perm = np.concatenate([c.astype(np.float32) for c in cols], 1)

    def level(n, m):
        a, b = np.arange(n)[:, None], np.arange(n)[None, :]
        return (a // (2 * m) == b // (2 * m)) & (a // m % 2 == 1) & (b // m % 2 == 0)

    t4 = np.arange(NS)
    s4 = (t4[:, None] // NSTEP) == (t4[None, :] // NSTEP)
    up, upi = t4[:, None] < t4[None, :], t4[:, None] <= t4[None, :]
    notstart = np.ones(T)
    notstart[0:SEQ:CH] = 0
    notstart[SEQ::NSTEP] = 0
    half = lambda m: np.tile(m, (2, 1))
    ci, cj = np.arange(CH)[:, None], np.arange(CH)[None, :]
    wkv = [same & (i < j), same & (i <= j), half(ci < cj)] + [half(level(CH, m)) for m in (2, 4, 8, 16, 32)]
    wkv += [half(level(CH, 1).T), half(np.eye(CH))]
    wkv += [np.tile(s4 & up, (4, 1)), np.tile(s4 & upi, (4, 1)), np.tile(level(NS, 1).T, (4, 1)),
            np.tile(level(NS, 2), (4, 1)), np.tile(np.eye(NS), (4, 1)),
            np.tile(t4[:, None] // NSTEP == np.arange(NSEQ)[None, :], (4, 1)), np.tile(notstart, (P, 1))]
    wkv = np.concatenate([c.astype(np.float32) for c in wkv], 1)
    inv = np.ones((4, 16), np.float32)
    for g in range(4):
        w = 2 << g
        inv[g] = w / np.minimum(w, np.arange(16) + 1).astype(np.float32)
    return perm, wkv, np.tile(inv.reshape(1, 64), (P, 1)).astype(np.float32)


NW = 256 + 8 * CH + 64 + 32 * 3 + 8 + T


class Chain:

    def __init__(self, eng, sem, per=0):
        self.eng, self.sem, self.per, self.i, self.n = eng, sem, per, 0, 0

    def turn(self, i):
        assert self.per == 0 or self.n in (0, self.per), self.n
        self.i, self.n = i, 0

    def __call__(self, ins):
        self.n += 1
        ins.then_inc(self.sem, 1)
        self.eng.wait_ge(self.sem, self.i * self.per + self.n)


def build(nc, x_prompt, x_sample, state_wkv, state_shift, state_pool, ln_g, ln_b, rw_mu, rw_wr, rw_wk, rw_wv,
          rw_wo, rw_w0, rw_w1, rw_w2, rw_a0, rw_a1, rw_a2, rw_g1, rw_g2, rw_kk, rw_ka, rw_rk, rw_gn_g, rw_gn_b,
          pool_w, pool_scale, ffn_w_in, ffn_w_down, c_perm, c_wkv, c_inv,
          y_prompt, y_sample, wkv_p, shift_p, pool_p, wkv_s, shift_s, pool_s):
    ctx = ExitStack()
    with ctx:
        base = (nc.sbuf_base + 31) // 32 * 32
        place = {}

        def at(name, shape, dt, offset):
            n = 4
            for s in shape[1:]:
                n *= s
            place[name] = (offset, offset + n)
            return nc.alloc_sbuf_tensor_at(name, shape, dt, offset=base + offset)

        def after(name):
            return place[name][1]

        def sem(name):
            return ctx.enter_context(nc.semaphore(name))

        RAW = at("RAW", [P, 4, 2048], F32, 0)
        WH = at("WH", [P, 2, 2048], F32R, after("RAW"))
        WL = at("WL", [P, 2, 2048], F32R, after("WH"))
        X = at("X", [P, KC, T + 1], F32, after("WL"))
        XPS = at("XPS", [P, KC, NS], F32, after("X"))
        PAR = at("PAR", [P, 3 * P], F32, after("XPS"))
        OMU = at("OMU", [P, 96], F32, after("PAR"))
        CP = at("CP", [P, 4 * P], F32, after("OMU"))
        TM = at("TM", [P, 2, T], F32, after("CP"))
        LHH = at("LHH", [P, 4, T], F32R, after("TM"))
        LHL = at("LHL", [P, 4, T], F32R, after("LHH"))
        MH = [None, None]
        ML = [None, None]
        MH[0] = at("MH0", [P, KC, T], F32R, after("LHL"))
        ML[0] = at("ML0", [P, KC, T], F32R, after("MH0"))
        MH[1] = at("MH1", [P, KC, T], F32R, after("ML0"))
        ML[1] = at("ML1", [P, KC, T], F32R, after("MH1"))
        R = at("R", [P, KC, T], F32, after("ML1"))
        K = at("K", [P, KC, T], F32, after("R"))
        assert base + after("K") <= nc.sbuf_usable_end, (base, after("K"), nc.sbuf_usable_end)
        XROW = at("XROW", [P, 2, 3, 512], F32, place["MH1"][0])
        PROW = at("PROW", [P, 3, P], F32, after("XROW"))
        V = at("V", [P, KC, T], F32, place["MH0"][0])
        SG = at("SG", [P, KC, T], F32, place["ML1"][0])
        A = at("A", [P, KC, T], F32, place["MH1"][0])
        KK = at("KK", [P, KC, T], F32, place["ML0"][0])
        off = [0]

        def ring(name, shape, dt=F32):
            t = at(name, shape, dt, off[0])
            off[0] = (place[name][1] + 31) // 32 * 32
            assert off[0] <= place["PAR"][0], (name, off[0])
            return t

        CW = ring("CW", [P, NW])
        TILES = dict(
            S0N=[P, 4, P], S0T=[P, NSEQ, HN],
            AR=[P, 2, T], BF=[P, T], KF=[P, T], VF=[P, T],
            CS=[P, T], CSX=[P, T], PC=[P, T],
            TOK=[P, 2, 4, P], TS=[P, 3, HN],
            RB=[P, 2, 2, P], MR=[P, 2, 2, 2 * P], LT=[P, 4, CH], SM=[P, 64],
            TT=[P, 2, 4, CH], XL=[P, 4, CH],
            STI=[P, NS], STT=[P, NS], SXL=[P, NS],
            MV=[P, 4, HN], WT=[P, 2, P], Q=[P, 4, HN],
            WR=[P, NSEQ, 8], QT=[P, NS], MVS=[P, HN], UT=[P, NS], YS=[P, NS], U=[P, 2, P],
            ST=[P, 2, HN], SPD=[P, HN], UVX=[P, NSEQ, HN], SOS=[P, 4, P], SOP=[HN, P])

        class Tiles:
            pass

        pairs = []
        for b in range(2):
            z = Tiles()
            tiles = {n: ring(f"{n}_{b}", shape) for n, shape in TILES.items()}
            (z.S0N, z.S0T, z.AR, z.BF, z.KF, z.VF, z.CS, z.CSX, z.PC, z.TOK, z.TS, z.RB, z.MR, z.LT, z.SM,
             z.TT, z.XL, z.STI, z.STT, z.SXL, z.MV, z.WT, z.Q, z.WR, z.QT, z.MVS, z.UT, z.YS, z.U, z.ST, z.SPD,
             z.UVX, z.SOS, z.SOP) = tiles.values()
            pairs.append(z)
        hid = place["MH1"][0]
        HH = at("HH", [P, HG, T], F32R, hid)
        HL = at("HL", [P, HG, T], F32R, after("HH"))
        assert after("HL") <= after("K")
        SQ = at("SQ", [P, KC, T], F32, hid)
        LNS = at("LNS", [P, 2, T], F32, after("SQ"))
        EP = [at("EP0", [P, KC, BUF + SEQ], F32, hid)]
        EP.append(at("EP1", [P, KC, BUF + SEQ], F32, after("EP0")))
        ES1 = at("ES1", [P, KC, NSEQ, BUF + NSTEP], F32, after("EP1"))
        ES = [at("ES0", [P, KC, NSEQ, BUF + NSTEP], F32, after("ES1")), ES1]
        assert place["ES0"][0] >= after("LNS")
        CI = at("CI", [P, 4, 16], F32, after("ES0"))
        DP = at("DP", [P, KC, T], F32, after("CI"))
        PAST = at("PAST", [P, D], F32, place["DP"][0])
        assert after("DP") <= after("K")
        TR = at("TR", [48, D], F32, place["MH0"][0])
        YROW = at("YROW", [P, 3, D], F32, place["LNS"][1])
        assert after("YROW") <= after("K")

        PS = [ctx.enter_context(nc.psum_tensor(f"PS{i}", [P, 512], F32)) for i in range(8)]

        SUM = at("SUM", [P, T], F32, place["LHH"][0])
        IDN = CP[:, 0:P]
        AVG = CP[:, P:2 * P]
        HEADS = CP[:, 2 * P:3 * P]
        HEADAVG = CP[:, 3 * P:4 * P]
        cm = [0]

        def cw(n):
            cm[0] += n
            return CW[:, cm[0] - n:cm[0]]

        M_PROD = cw(256)
        M_CHUNK = cw(CH)
        M_LEVEL = [cw(CH) for _ in range(5)]
        M_ONE = cw(CH)
        IDC = cw(CH)
        MS_PROD = cw(64)
        MS_ONE = cw(NS)
        MS_TWO = cw(NS)
        IDS = cw(NS)
        MS_SEQ = cw(NSEQ)
        NOTSTART = cw(T)
        assert cm[0] == NW
        for b, z in enumerate(pairs):
            z.b, z.B, z.YT = b, PS[4 * b:4 * b + 4], TM[:, b, :]

        def one(t, c):
            return t[:, bass.ds(c, 1), :].rearrange("p a t -> p (a t)")

        def chunk(z, i):
            return 2 * i + z.b

        def par(name, c):
            return PAR[:, bass.ds(PCOL[name] + c, 1)]

        const_in = sem("const_in")
        prow_in = sem("prow_in")
        xrow_in = [sem(f"xrow_in{i}") for i in range(2)]
        x_turned = sem("x_turned")
        x_bank_free = sem("x_bank_free")
        par_turned = sem("par_turned")
        par_ready = sem("par_ready")
        x_ready = sem("x_ready")
        omu_ready = sem("omu_ready")
        raw_landed = [sem(f"raw_landed{i}") for i in range(4)]
        hi_ready = sem("hi_ready")
        lo_ready = sem("lo_ready")
        slab_used = sem("slab_used")
        row_ready = sem("row_ready")
        out_free = sem("out_free")
        tm_ready = sem("tm_ready")
        mt_ready = sem("mt_ready")
        mixhi_ready = sem("mixhi_ready")
        mixlo_ready = sem("mixlo_ready")
        lh_ready = sem("lh_ready")
        lhh_ready = sem("lhh_ready")
        lhl_ready = sem("lhl_ready")
        kc_ready = sem("kc_ready")
        kks_ready = sem("kks_ready")
        kkn_ready = sem("kkn_ready")
        kkd_ready = sem("kkd_ready")
        kk_ready = sem("kk_ready")
        kk_self = sem("kk_self")
        wkv_go = sem("wkv_go")
        wkv_const = sem("wkv_const")
        wkv_done = sem("wkv_done")
        yg_ready = sem("yg_ready")
        ygh_ready = sem("ygh_ready")
        ygl_ready = sem("ygl_ready")
        sg_ready = sem("sg_ready")
        hid_ready = sem("hid_ready")
        hh_ready = sem("hh_ready")
        hl_ready = sem("hl_ready")
        hid_self = sem("hid_self")
        stores = sem("stores")
        final_stores = sem("final_stores")

        levels = [f"{n}{lv}" for lv in range(5) for n in ("x", "t")]
        later = [f"{n}{c}" for c in range(1, 4) for n in ("u", "s")]
        PE_STEPS = (["s0", "tok", "prod", "two"] + levels + ["q", "s0c"] + later + ["y"])
        DVE_STEPS = (["cs", "csx", "kt", "kt2", "bfa", "rkp", "feats", "sm", "tit", "stt", "two", "masks"]
                     + levels[:6] + ["utc", "uvx"] + levels[6:8] + ["snw", "snw2"] + levels[8:]
                     + ["bonv", "st0"]
                     + [f"{n}{c}" for c in range(1, 4) for n in ("spd", "u", "st")]
                     + ["yr", "yout"])
        ACT_STEPS = ["decays", "s0t", "tok", "two", "wr", "qt", "sos", "mv", "q", "sop"]
        NORM_STEPS = dict(pe=["mean", "var"], dve=["cen", "rstd", "norm", "scale", "done"], act=["sq", "var", "sd"])

        class Steps:

            def __init__(self, name, steps, b):
                assert len(set(steps)) == len(steps)
                self.sem, self.steps, self.n, self.at = sem(f"{name}_pair{b}"), steps, len(steps), 0

            def done(self, ins, step):
                assert self.steps[self.at % self.n] == step, (step, self.steps[self.at % self.n])
                self.at += 1
                ins.then_inc(self.sem, 1)

            def value(self, step, i, turn=0):
                return self.n * (i + turn + 1) + self.steps.index(step) + 1 if isinstance(i, int) else \
                    i * self.n + (self.n * (turn + 1) + self.steps.index(step) + 1)

        for b, z in enumerate(pairs):
            z.pe, z.dve, z.act = Steps("pe", PE_STEPS, b), Steps("dve", DVE_STEPS, b), Steps("act", ACT_STEPS, b)
            z.npe, z.ndve, z.nact = (Steps("norm_" + n, steps, b) for n, steps in NORM_STEPS.items())
            z.s0in, z.stored, z.store_done = sem(f"s0in{b}"), sem(f"stored{b}"), sem(f"store_done{b}")
        xkept = sem("xkept")
        xback = sem("xback")
        XKEEP = nc.dram_tensor("x_keep", [P, KC, T], F32, kind="Internal").ap()

        FRONT, BACK, NORM = 0, 1, 2
        LEVELS = [range(3), range(3, 5)]
        PHASES = [11, 13, 5]

        def weave(program, *parts):
            at, running = [], []
            for q, (b, i, part, *normed) in enumerate(parts):
                at += [((n + (0.8 if part == BACK else 0.5)) / PHASES[part], q) for n in range(PHASES[part])]
                running.append(program(pairs[b], 2 * i + b, i, part, normed[0] if normed else None))
            for _, q in sorted(at):
                next(running[q])
            assert all(next(q, None) is None for q in running)

        def turns(eng, program):
            last = KC // 2 - 1
            weave(program, (0, 0, FRONT))
            weave(program, (0, 0, BACK), (1, 0, FRONT))
            with eng.Fori(0, last) as i:
                weave(program, (1, i, BACK), (0, i + 1, FRONT, i))
                weave(program, (0, i + 1, BACK), (1, i + 1, FRONT, i))
            weave(program, (1, last, BACK), (0, last, NORM, last))
            weave(program, (1, last, NORM, last))

        ln = {n: sem("ln_" + n) for n in ("x", "mean", "cen", "sq", "var", "sd", "rstd", "scaled", "done", "lo")}
        HALVED = {0: 0, 2: KC}
        pl = {n: sem("pool_" + n) for n in ("pastT", "past", "ext", "d", "hi", "lo", "scaled", "trT", "self", "es")}
        tr_stored = sem("tr_stored")
        yt = {n: sem("yt_" + n) for n in ("T", "free")}

        block = ctx.enter_context(nc.Block())

        @block.sync
        def _(sp):
            sp.dma_start(CP[:, :], c_perm).then_inc(const_in, 16)
            rows = lambda a: a.rearrange("(c p) -> c p", p=P)
            prow = [(0, 96, rw_mu.rearrange("n j (c p) -> (n j c) p", p=P)), (96, 16, rows(rw_w0[0])),
                    (112, 16, rows(rw_a0[0])), (128, 16, rows(rw_kk[0])), (144, 16, rows(rw_ka[0])),
                    (160, 16, rw_rk.rearrange("n (c e) v -> (n c) (e v)", e=2)), (176, 16, rows(rw_gn_g[0])),
                    (192, 16, rows(rw_gn_b[0])), (208, 16, rows(pool_scale[0])),
                    (256, 64, ln_g.rearrange("a b (c p) -> (a b c) p", p=P)),
                    (320, 64, ln_b.rearrange("a b (c p) -> (a b c) p", p=P))]
            for col, n, src in prow:
                sp.dma_start(PROW[col % P:col % P + n, col // P, :], src).then_inc(prow_in, 16)
            with sp.Fori(0, 2) as i:
                for b in range(2):
                    sp.wait_ge(x_turned, 8 * i + 4 * b + 4)
                    cols = bass.ds((2 * i + b) * 512, 512)
                    sp.dma_start(XROW[:, b, 0:2, :], x_prompt[0][:, cols].rearrange("(a p) n -> p a n", p=P))\
                      .then_inc(xrow_in[b], 16)
                    sp.dma_start(XROW[0:NS, b, 2, :], x_sample.rearrange("b t d -> (b t) d")[:, cols])\
                      .then_inc(xrow_in[b], 16)
                    sp.dma_start(XROW[NS:NS + NSEQ, b, 2, :], state_shift[0][:, cols]).then_inc(xrow_in[b], 16)

            def slab(s, slot, dst, src):
                sp.wait_ge(lo_ready, s + 1)
                sp.dma_start(dst, src).then_inc(raw_landed[slot], 16)

            def square(s0, wt):
                with sp.Fori(0, 4) as i:
                    for j in range(4):
                        slab(s0 + 4 * i + j, j, RAW[:, j, :].rearrange("p (k m) -> p k m", k=KC),
                             wt[:, bass.ds((4 * i + j) * P, P)].rearrange("(k p) m -> p k m", p=P))

            s = SLAB["lora1"]
            for j, src in enumerate((rw_w1[0], rw_a1[0])):
                slab(s + j, j, RAW[:, j, 0:KC * DL].rearrange("p (k m) -> p k m", k=KC),
                     src.rearrange("(k p) m -> p k m", p=P))
            for j in range(2):
                slab(s + 2 + j, 2 + j, RAW[:, 2 + j, :].rearrange("p (k m) -> p k m", k=KC),
                     rw_g1[0][:, j * P:(j + 1) * P].rearrange("(k p) m -> p k m", p=P))
            square(SLAB["r"], rw_wr[0])
            square(SLAB["k"], rw_wk[0])
            square(SLAB["v"], rw_wv[0])
            s = SLAB["lora2"]
            slab(s, 0, RAW[0:DL, 0, :], rw_w2[0])
            slab(s + 1, 1, RAW[0:DL, 1, :], rw_a2[0])

            sp.wait_ge(x_ready, KC)
            sp.dma_start(XKEEP, X[:, :, 1:T + 1]).then_inc(xkept, 16)
            sp.wait_ge(wkv_go, 2)
            sp.wait_ge(xkept, 16)
            sp.dma_start(CW[:, :], c_wkv).then_inc(wkv_const, 16)
            with sp.Fori(0, KC // 2) as i:
                for b, z in enumerate(pairs):
                    sp.wait_ge(z.pe.sem, z.pe.value("s0", i, -1))
                    for b2 in range(2):
                        for h in range(2):
                            src = state_wkv[0].rearrange("(b c) h v k -> c v b h k", c=2)[b2]
                            src = src[:, :, bass.ds(4 * i + 2 * b + h, 1), :]
                            sp.dma_start(z.S0N[b2 * HN:(b2 + 1) * HN, :, h * HN:(h + 1) * HN],
                                         src.rearrange("v b h k -> v b (h k)")).then_inc(z.s0in, 16)

            assert place["S0N_1"][0] >= place["RAW"][1]
            sp.wait_ge(pairs[0].ndve.sem, pairs[0].ndve.value("done", KC // 2 - 1))
            sp.wait_ge(pairs[0].store_done, KC // 2 + 1)
            s = SLAB["g2"]
            for j in range(2):
                slab(s + j, 2 + j, RAW[:, 2 + j, :], rw_g2[0][j * P:(j + 1) * P, :])
            sp.wait_ge(wkv_done, 3)
            square(SLAB["o"], rw_wo[0])

            def ffn(layer):
                w_in = ffn_w_in[layer]
                w_down = ffn_w_down[layer]
                for g in range(2):
                    s = SLAB[f"ffn{layer}"] + g * FFN_SLABS
                    with sp.Fori(0, HG // 2) as i:
                        for j in range(4):
                            c = FC * (j % 2) + g * HG + 2 * i + j // 2
                            slab(s + 4 * i + j, j, RAW[:, j, :].rearrange("p (k m) -> p k m", k=KC),
                                 w_in[:, bass.ds(c * P, P)].rearrange("(k p) m -> p k m", p=P))
                    with sp.Fori(0, KC // 2) as i:
                        for j in range(4):
                            r0 = (g * HG + (j % 2) * HH2) * P
                            slab(s + 2 * HG + 4 * i + j, j,
                                 RAW[:, j, 0:HH2 * P].rearrange("p (k m) -> p k m", k=HH2),
                                 w_down[r0:r0 + HH2 * P, bass.ds((2 * i + j // 2) * P, P)]
                                 .rearrange("(k p) m -> p k m", p=P))

            ffn(0)
            for j in range(4):
                slab(SLAB["pool"] + j, j, RAW[:, j, :].rearrange("p (k m) -> p k m", k=4),
                     pool_w[0, j].rearrange("(k p) m -> p k m", p=P))
            ffn(1)

        past_go, past_in, inv_in, tr_ready = sem("past_go"), sem("past_in"), sem("inv_in"), sem("tr_ready")
        yrow_ready = sem("yrow_ready")

        @block.gpsimd
        def _(pool):
            pool.sem_inc(x_turned, 8)
            pool.sem_inc(x_bank_free, 4)
            pool.sem_inc(lo_ready, 4)
            pool.sem_inc(slab_used, 2)
            pool.sem_inc(out_free, 4)
            pool.sem_inc(mixlo_ready, 2)
            pool.sem_inc(hl_ready, 2)
            for z in pairs:
                for steps in (z.pe, z.dve, z.act, z.npe, z.ndve, z.nact):
                    pool.sem_inc(steps.sem, steps.n)
                pool.sem_inc(z.store_done, 1)
            pool.sem_inc(kk_ready, 2)
            pool.dma_start(shift_p[0], x_prompt[0, SEQ - 1:SEQ, :]).then_inc(stores, 16)
            pool.dma_start(shift_s[0], x_sample[:, NSTEP - 1, :]).then_inc(stores, 16)
            pool.dma_start(pool_s[0][:, 0:BUF - NSTEP, :], state_pool[0][:, NSTEP:BUF, :]).then_inc(stores, 16)
            for q in range(4):
                for c in range(KC):
                    pool.wait_ge(mixhi_ready, q * KC + c + 1)
                    pool.tensor_tensor(ML[q % 2][:, c, :], K[:, c, :], MH[q % 2][:, c, :].bitcast(F32), ALU.subtract)\
                        .then_inc(mixlo_ready, 1)
            with pool.Fori(0, KC // 2) as i:
                for b, z in enumerate(pairs):
                    value = pool.to_reg(z.act.value("sos", i))
                    pool.wait_ge(const_in, 16)
                    pool.wait_ge(z.act.sem, value)
                    for b2 in range(2):
                        for h in range(2):
                            dst = wkv_s[0].rearrange("(b c) h v k -> c v b h k", c=2)[b2]
                            dst = dst[:, :, bass.ds(4 * i + 2 * b + h, 1), :]
                            pool.dma_start(dst.rearrange("v b h k -> v b (h k)"),
                                           z.SOS[b2 * HN:(b2 + 1) * HN, :, h * HN:(h + 1) * HN])\
                                .then_inc(z.stored, 16)
                    value = pool.to_reg(z.act.value("sop", i))
                    pool.wait_ge(const_in, 16)
                    pool.wait_ge(z.act.sem, value)
                    pool.dma_start(wkv_p[0, 0].rearrange("h v k -> v h k")[:, bass.ds(4 * i + 2 * b, 2), :],
                                   z.SOP[:, :].rearrange("v (h k) -> v h k", h=2)).then_inc(z.stored, 16)
                    pool.wait_ge(z.stored, 80 * i + 80)
                    pool.sem_inc(z.store_done, 1)
            pool.sem_inc(wkv_done, 1)
            pool.wait_ge(wkv_done, 3)
            pool.wait_ge(hi_ready, SLAB["o"] + 2)
            pool.dma_start(X[:, :, 1:T + 1], XKEEP).then_inc(xback, 16)

            def sums(k, ready, at):
                for c in range(KC):
                    pool.wait_ge(ready, at + c + 1)
                    if c == 0:
                        if k:
                            pool.wait_ge(ln["mean"], k)
                        ins = pool.tensor_copy(SUM[:, :], X[:, 0, 1:T + 1])
                    else:
                        pool.wait_ge(ln["x"], KC * k + c)
                        ins = pool.tensor_tensor(SUM[:, :], SUM[:, :], X[:, c, 1:T + 1], ALU.add)
                    ins.then_inc(ln["x"], 1)

            sums(0, out_free, 4 + OUT["o"])
            sums(1, out_free, 4 + OUT["ffn0"] + 2 * FFN_OUTS - KC)
            pool.wait_ge(past_go, 2)
            pool.dma_start(PAST[0:NSEQ * BUF, :], state_pool[0].rearrange("b t d -> (b t) d")).then_inc(past_in, 16)
            pool.dma_start(CI[:, :, :], c_inv.rearrange("p (g t) -> p g t", g=4)).then_inc(inv_in, 16)
            pool.wait_ge(ln["done"], 2 * KC)

            def window(lv, c0, c1):
                d, m = 1 << lv, (2 << lv) - 1
                a, b = [ES[n][:, c0:c1, :, :].rearrange("p c b t -> p (c b) t") for n in (lv % 2, (lv + 1) % 2)]
                pool.tensor_tensor(b[:, :, m:], a[:, :, m:], a[:, :, m - d:BUF + NSTEP - d], ALU.add)\
                    .then_inc(pl["es"], 1)

            for n, (c0, c1) in enumerate(((0, 4), (4, KC))):
                pool.wait_ge(pl["past"], c1 // 4)
                for c in range(c0, c1):
                    ins = pool.tensor_copy(ES[0][:, c, :, BUF:],
                                           X[:, c, SEQ + 1:T + 1].rearrange("p (b t) -> p b t", b=NSEQ))
                ins.then_inc(pl["es"], 1)
                pool.wait_ge(pl["es"], 2 * n + 1)
                window(0, c0, c1)
            for lv in range(1, 4):
                pool.wait_ge(pl["es"], lv + 3)
                window(lv, 4 * lv, KC)
            pool.wait_ge(stores, 16 * 3)
            sums(2, pl["scaled"], 2)
            sums(3, out_free, 4 + OUT["ffn1"] + 2 * FFN_OUTS - KC)
            for q in range(4):
                cs = slice(q * 512, (q + 1) * 512)
                pool.wait_ge(yrow_ready, 3 * q + 3)
                pool.dma_start(y_prompt[0].rearrange("(a p) d -> p a d", p=P)[:, :, cs], YROW[:, 0:2, cs])\
                    .then_inc(final_stores, 16)
                pool.dma_start(y_sample.rearrange("b t d -> (b t) d")[:, cs], YROW[0:NS, 2, cs])\
                    .then_inc(final_stores, 16)
            pool.wait_ge(final_stores, 16 * 8)

        @block.tensor
        def _(pe):
            def three(out, wh, wl, xh, xl, first, last):
                pe.matmul(out, wh, xh, start=first, stop=False)
                pe.matmul(out, wh, xl, start=False, stop=False)
                return pe.matmul(out, wl, xh, start=False, stop=last)

            def take_slab(s):
                pe.wait_ge(lo_ready, s + 5)

            def take_bank(o):
                pe.wait_ge(out_free, o + 1)

            pe.wait_ge(const_in, 16)
            pe.wait_ge(prow_in, 16 * 11)
            for g, n in ((0, 128), (1, 96), (2, 128)):
                ins = pe.transpose(PS[4][:, g * P:g * P + n], PROW[0:n, g, :], CP[0:n, 0:n])
            ins.then_inc(par_turned, 1)
            with pe.Fori(0, 2) as i:
                for b in range(2):
                    pe.wait_ge(xrow_in[b], 48 * i + 48)
                    for c in range(4):
                        pe.wait_ge(x_bank_free, (2 * i + b) * 4 + c + 1)
                        for a, (n, m) in enumerate(((P, P), (P, P), (NS + NSEQ, NS + NSEQ))):
                            ins = pe.transpose(PS[c][:, a * P:a * P + n], XROW[0:n, b, a, c * P:(c + 1) * P],
                                               CP[0:n, 0:n])
                        ins.then_inc(x_turned, 1)

            for j, (name, wd) in enumerate((("w", DL), ("a", DL), ("g", P), ("g", P))):
                s, o = SLAB["lora1"] + j, OUT["lora1"] + j
                take_slab(s)
                take_bank(o)
                if j == 0:
                    pe.wait_ge(x_bank_free, 20)
                q, m = MIX[name], MIX[name] % 2
                for k in range(KC):
                    if j < 3:
                        pe.wait_ge(mixlo_ready, 2 + q * KC + k + 1)
                    ins = three(PS[o % 4][0:wd, 0:T], WH[:, s % 2, k * wd:(k + 1) * wd], WL[:, s % 2, k * wd:(k + 1) * wd],
                                MH[m][:, k, :], ML[m][:, k, :], k == 0, k == KC - 1)
                ins.then_inc(slab_used, 1)

            def square(name, xh, xl, ready, at, extra=None, pair=False):
                s0, o0 = SLAB[name], OUT[name]

                def step(j, k):
                    return three(PS[j][:, 0:T], WH[:, j % 2, k * P:(k + 1) * P], WL[:, j % 2, k * P:(k + 1) * P],
                                 xh[:, k, :], xl[:, k, :], k == 0, k == KC - 1)

                def outputs(i, js, await_input=False):
                    for j in js:
                        take_slab(s0 + 4 * i + j)
                        take_bank(o0 + 4 * i + j)
                    for k in range(KC):
                        if await_input:
                            pe.wait_ge(ready, at + k + 1)
                        last = [step(j, k) for j in js]
                    for ins in last:
                        ins.then_inc(slab_used, 1)
                    if extra is not None:
                        for j in js:
                            extra(i, j)

                n = 2 if pair else 1
                outputs(0, range(n), True)
                for j in range(n, 4):
                    outputs(0, [j])
                with pe.Fori(1, 4) as i:
                    for j in range(4):
                        outputs(i, [j])

            for name in ("r", "k"):
                q = MIX[name]
                square(name, MH[q % 2], ML[q % 2], mixlo_ready, 2 + q * KC, pair=name == "r")

            def key_norms(i, j):
                pe.wait_ge(kks_ready, 4 * i + j + 1)
                pe.matmul(PS[4 + j % 2][:, 0:T], HEADS, TM[:, j % 2, :], start=True, stop=True).then_inc(kkn_ready, 1)

            square("v", MH[1], ML[1], mixlo_ready, 2 + 5 * KC, key_norms)

            pe.wait_ge(lhl_ready, 4)
            for j in range(2):
                s = SLAB["lora2"] + j
                take_slab(s)
                for m in range(KC):
                    o = OUT["lora2"] + j * KC + m
                    take_bank(o)
                    ins = three(PS[o % 4][:, 0:T], WH[0:DL, j, m * P:(m + 1) * P], WL[0:DL, j, m * P:(m + 1) * P],
                                LHH[0:DL, j, :], LHL[0:DL, j, :], True, True)
                    ins.then_inc(row_ready, 1)
                pe.drain().then_inc(slab_used, 1)
            pe.sem_inc(wkv_go, 1)

            pe.wait_ge(wkv_const, 16)
            pe.wait_ge(out_free, 4 + OUT["g2"])
            hr = [slice(0, HN), slice(HN, P)]

            def lo32(h):
                return slice(h * HN, h * HN + 32)

            def hi32(h):
                return slice(h * HN + 32, h * HN + 64)

            def await_step(steps, step, i, turn=0):
                value = steps.value(step, i, turn)
                if not isinstance(i, int):
                    value = pe.to_reg(value)
                    pe.wait_ge(const_in, 16)
                pe.wait_ge(steps.sem, value)

            def pair(z, p, i, part, done):
                B = z.B
                blocks = [(t, h, r) for t in range(2) for h in range(2) for r in range(2)]

                def norm(step):
                    if done is None:
                        return
                    y = one(R, chunk(z, done))
                    if step == "mean":
                        await_step(z.dve, "yout", done)
                        z.npe.done(pe.matmul(B[2][:, 0:T], HEADAVG, y, start=True, stop=True), "mean")
                    if step == "var":
                        await_step(z.nact, "sq", done)
                        z.npe.done(pe.matmul(B[3][:, 0:T], HEADAVG, z.YT, start=True, stop=True), "var")

                if part == NORM:
                    norm("mean")
                    yield
                    yield
                    norm("var")
                    yield
                    yield
                    yield
                    return

                def blockwise(bank, col, lhs, rhs):
                    for t, h, r in blocks:
                        u = 2 * t + h
                        ins = pe.matmul(B[bank][hr[r], col + u * CH:col + (u + 1) * CH], lhs(hr[r], u), rhs(hr[r], u),
                                        start=True, stop=True)
                    return ins

                if part == FRONT:
                    norm("mean")
                    pe.wait_ge(z.s0in, 64 * i + 64)
                    await_step(z.dve, "yout", i, -1)
                    for b in range(4):
                        ins = pe.transpose(B[0][:, b * P:(b + 1) * P], z.S0N[:, b, :], IDN)
                    z.pe.done(ins, "s0")
                    yield
                    norm("var")
                    yield
                    await_step(z.ndve, "cen", i, -1)
                    await_step(z.nact, "var", i, -1)
                    await_step(z.act, "decays", i)
                    await_step(z.dve, "feats", i)
                    feats = [z.AR[:, 0, :], z.BF[:, :], z.KF[:, :], z.VF[:, :]]
                    for t in range(2):
                        for n, f in enumerate(feats):
                            pe.transpose(B[1 + t][:, n * P:(n + 1) * P], f[:, t * P:(t + 1) * P], IDN)
                    for h in range(2):
                        for n, (f, y) in enumerate(((0, 0), (0, 1), (1, 0), (2, 1), (3, 0), (3, 1))):
                            ins = pe.matmul(B[3][h * HN + 32 * y:h * HN + 32 * y + 32, (n // 2) * HN:(n // 2 + 1) * HN],
                                            feats[f][hr[h], SEQ:T], CP[hr[h], hr[h]], start=True, stop=True)
                    z.pe.done(ins, "tok")
                    yield
                    await_step(z.act, "tok", i)
                    for t in range(2):
                        for h in range(2):
                            ts = slice(t * P, (t + 1) * P)
                            pe.matmul(B[3 * h][:, ts], z.BF[hr[h], ts], z.AR[hr[h], 1, ts], start=True, stop=True)
                    for t in range(2):
                        for h in range(2):
                            for r in range(2):
                                cs = slice(t * P + r * CH, t * P + (r + 1) * CH)
                                pe.matmul(B[3 * h][hr[r], 256 + t * CH:256 + (t + 1) * CH], z.BF[hr[h], cs],
                                          z.AR[hr[h], 0, cs], start=True, stop=True)
                    for h in range(2):
                        for y, f in ((0, z.BF), (1, z.KF)):
                            pe.matmul(B[0][h * HN + 32 * y:h * HN + 32 * y + 32, 384:448], f[hr[h], SEQ:T],
                                      z.AR[hr[h], :, SEQ:T], start=True, stop=True)
                    for t in range(2):
                        for h in range(2):
                            ins = pe.matmul(B[1 + h][:, t * 256:(t + 1) * 256], z.KF[hr[h], t * P:(t + 1) * P],
                                            z.AR[hr[h], :, t * P:(t + 1) * P], start=True, stop=True)
                    z.pe.done(ins, "prod")
                    yield
                    await_step(z.dve, "two", i)
                    blockwise(0, 0, lambda q, u: z.TT[q, 1, u, :], lambda q, u: IDC[q, :])
                    for h in range(2):
                        ins = pe.matmul(B[3][lo32(h), 0:NS], z.STT[lo32(h), :], IDS[lo32(h), :], start=True, stop=True)
                    z.pe.done(ins, "two")
                    yield
                for lv in LEVELS[part]:
                    if lv == 0:
                        await_step(z.dve, "masks", i)
                    await_step(*((z.act, "two", i) if lv == 0 else (z.dve, f"t{lv - 1}", i)))
                    ins = blockwise(1, 0, lambda q, u: z.LT[q, u, :], lambda q, u: z.TT[q, 0, u, :])
                    if lv == 0:
                        for h in range(2):
                            ins = pe.matmul(B[3][lo32(h), 64:64 + NS], z.SM[lo32(h), 0:NS], z.STI[lo32(h), :],
                                            start=True, stop=True)
                    if lv == 1:
                        for h in range(2):
                            pe.matmul(B[3][lo32(h), 128:128 + HN], z.SM[hi32(h), 0:NS], z.TS[hi32(h), 2, :],
                                      start=True, stop=True)
                        for h in range(2):
                            ins = pe.matmul(B[3][hr[h], 192:192 + NS], z.TS[lo32(h), 0, :], z.STT[lo32(h), :],
                                            start=True, stop=True)
                    if lv == 2:
                        await_step(z.act, "wr", i)
                        for h in range(2):
                            for b in range(NSEQ):
                                ins = pe.matmul(B[0][hr[h], b * 8:(b + 1) * 8], z.S0T[hr[h], b, :], z.WR[hr[h], b, :],
                                                start=True, stop=True)
                    if lv == 3:
                        await_step(z.dve, "uvx", i)
                        for h in range(2):
                            ins = pe.matmul(B[0][hr[h], :], z.TS[hr[h], 1, :], z.UVX[hr[h], :, :],
                                            start=True, stop=True)
                    if lv == 4:
                        await_step(z.dve, "snw2", i)
                        for b in range(4):
                            ins = pe.transpose(B[0][:, b * P:(b + 1) * P], z.UVX[:, 2 * b:2 * b + 2, :], IDN)
                    z.pe.done(ins, f"x{lv}")
                    yield
                    await_step(z.dve, f"x{lv}", i)
                    if lv < 4:
                        ins = blockwise(2, 0, lambda q, u: z.TT[q, 1, u, :], lambda q, u: z.XL[q, u, :])
                    ins = blockwise(2, 256, lambda q, u: z.XL[q, u, :], lambda q, u: z.TT[q, 1, u, :])
                    if lv == 0:
                        for h in range(2):
                            ins = pe.matmul(B[3][lo32(h), 96:96 + NS], z.SXL[lo32(h), :], z.STT[lo32(h), :],
                                            start=True, stop=True)
                    if lv == 1:
                        await_step(z.act, "wr", i)
                        for h in range(2):
                            ins = pe.matmul(B[3][hr[h], 224:224 + NS], z.MVS[lo32(h), :], z.STT[lo32(h), :],
                                            start=True, stop=True)
                    if lv == 2:
                        for h in range(2):
                            ins = pe.matmul(B[3][lo32(h), 256:256 + HN], z.UT[hr[h], :], CP[hr[h], hr[h]],
                                            start=True, stop=True)
                    if lv == 4:
                        for t in range(2):
                            for h in range(2):
                                u = 2 * t + h
                                ins = pe.matmul(B[3][:, u * HN:(u + 1) * HN], z.MR[:, t, h, 0:P], z.TOK[:, t, 3, hr[h]],
                                                start=True, stop=True)
                    z.pe.done(ins, f"t{lv}")
                    yield
                if part == FRONT:
                    return
                await_step(z.act, "mv", i)
                await_step(z.dve, "t4", i)
                for t, h, r in blocks:
                    pe.matmul(B[1 - r][hr[h], t * CH:(t + 1) * CH], z.TOK[hr[r], t, 0, hr[h]],
                              z.TT[hr[r], 1, 2 * t + h, :], start=True, stop=True)
                blockwise(2, 0, lambda q, u: z.TT[q, 1, u, :], lambda q, u: z.MV[q, u, :])
                ins = pe.matmul(B[1][:, 128:128 + T], HEADS, one(SG, p), start=True, stop=True)
                z.pe.done(ins, "q")
                yield
                await_step(z.act, "q", i)
                col = lambda t, r: slice(128 + t * P + r * CH, 128 + t * P + (r + 1) * CH)

                def state(c):
                    t, rr = c // 2, hr[c % 2]
                    for h in range(2):
                        pe.matmul(B[3][hr[h], 256:256 + HN], z.TOK[rr, t, 1, hr[h]], z.U[rr, t, hr[h]],
                                  start=True, stop=False)
                        ins = pe.matmul(B[3][hr[h], 256:256 + HN], z.TOK[rr, t, 2, hr[h]], z.TOK[rr, t, 3, hr[h]],
                                        start=False, stop=True)
                    return ins

                z.pe.done(state(0), "s0c")
                for h in range(2):
                    pe.matmul(B[0][hr[h], 128:256], z.TOK[:, 0, 3, hr[h]], z.MR[:, 0, h, P:2 * P], start=True,
                              stop=False)
                yield
                for c in range(1, 4):
                    t, rr = c // 2, hr[c % 2]
                    await_step(z.dve, f"st{c - 1}", i)
                    for h in range(2):
                        ins = pe.matmul(B[1 + h][rr, 448:512], z.WT[hr[h], t, rr], z.ST[hr[h], c % 2, :],
                                        start=True, stop=True)
                    z.pe.done(ins, f"u{c}")
                    if c == 2:
                        for h in range(2):
                            pe.matmul(B[0][hr[h], 256:384], z.TOK[:, 1, 3, hr[h]], z.MR[:, 1, h, P:2 * P], start=True,
                                      stop=False)
                    for h in range(2):
                        pe.matmul(B[0][hr[h], col(t, c % 2)], z.ST[hr[h], c % 2, :],
                                  z.AR[hr[h], 1, c * CH:(c + 1) * CH], start=False, stop=False)
                    yield
                    await_step(z.dve, f"u{c}", i)
                    z.pe.done(state(c), f"s{c}")
                    if c % 2:
                        for h in range(2):
                            pe.matmul(B[0][hr[h], 128 + t * P:128 + (t + 1) * P], z.U[:, t, hr[h]], z.RB[:, t, h, :],
                                      start=False, stop=True)
                    yield
                for h in range(2):
                    pe.matmul(B[0][hr[h], 384:384 + NS], z.TS[hr[h], 2, :], z.SM[hr[h], 32:64], start=True, stop=True)
                await_step(z.dve, "st3", i)
                ins = pe.transpose(B[3][0:HN, 320:320 + P], z.ST[:, 0, :], IDN)
                z.pe.done(ins, "y")
                yield

            turns(pe, pair)
            for z in pairs:
                pe.wait_ge(z.ndve.sem, z.ndve.value("done", KC // 2 - 1))
            pe.sem_inc(wkv_done, 1)

            for j in range(2):
                take_slab(SLAB["g2"] + j)
            for m in range(KC):
                o = OUT["g2"] + m
                take_bank(o)
                for j in range(2):
                    ins = three(PS[o % 4][:, 0:T], WH[:, j, m * P:(m + 1) * P], WL[:, j, m * P:(m + 1) * P],
                                LHH[:, 2 + j, :], LHL[:, 2 + j, :], j == 0, j == 1)
                ins.then_inc(row_ready, 1)
            pe.drain().then_inc(slab_used, 2)
            square("o", MH[0], ML[0], ygl_ready, 0)

            def layer_norm(k):
                pe.wait_ge(ln["x"], KC * (k + 1))
                pe.matmul(PS[4][:, 0:T], AVG, SUM[:, :], start=True, stop=True).then_inc(ln["mean"], 1)
                for q in range(4):
                    pe.wait_ge(ln["sq"], 4 * k + q + 1)
                    for c in range(4 * q, 4 * q + 4):
                        ins = pe.matmul(PS[5][:, 0:T], AVG, SQ[:, c, :], start=c == 0, stop=c == KC - 1)
                ins.then_inc(ln["var"], 1)

            def ffn(layer, lnk):
                for g in range(2):
                    s0 = SLAB[f"ffn{layer}"] + g * FFN_SLABS
                    o0 = OUT[f"ffn{layer}"] + g * FFN_OUTS
                    pe.wait_ge(out_free, o0 + 4)

                    def up(j, k):
                        return three(PS[j][:, 0:T], WH[:, j % 2, k * P:(k + 1) * P], WL[:, j % 2, k * P:(k + 1) * P],
                                     MH[0][:, k, :], ML[0][:, k, :], k == 0, k == KC - 1)

                    def hidden(i, j):
                        take_slab(s0 + 4 * i + j)
                        take_bank(o0 + 4 * i + j)
                        for k in range(KC):
                            ins = up(j, k)
                        ins.then_inc(slab_used, 1)

                    if g == 0:
                        take_slab(s0 + 1)
                        take_bank(o0 + 1)
                        for k in range(KC):
                            pe.wait_ge(ln["lo"], HALVED[lnk] + k + 1)
                            first = up(0, k)
                            second = up(1, k)
                        first.then_inc(slab_used, 1)
                        second.then_inc(slab_used, 1)
                        for j in (2, 3):
                            hidden(0, j)
                    with pe.Fori(1 - g, HG // 2) as i:
                        for j in range(4):
                            hidden(i, j)
                    s1, o1 = s0 + 2 * HG, o0 + 2 * HG
                    hidden_before = 2 + (2 * layer + g) * HG
                    pe.wait_ge(hl_ready, hidden_before + HH2)
                    with pe.Fori(0, KC // 2) as i:
                        for j in range(4):
                            take_slab(s1 + 4 * i + j)
                            if j % 2 == 0:
                                pe.wait_ge(out_free, o1 + 2 * i + j // 2 + 3)
                            elif j == 1:
                                pe.wait_ge(hl_ready, hidden_before + HG)
                            for k in range(HH2):
                                kk = (j % 2) * HH2 + k
                                ins = three(PS[j // 2][:, 0:T], WH[:, j % 2, k * P:(k + 1) * P],
                                            WL[:, j % 2, k * P:(k + 1) * P], HH[:, kk, :], HL[:, kk, :],
                                            kk == 0, kk == HG - 1)
                            ins.then_inc(slab_used, 1)

            layer_norm(0)
            ffn(0, 0)
            layer_norm(1)
            pe.wait_ge(past_in, 16)
            for c in range(KC):
                if c % 4 == 0 and c >= 8:
                    pe.wait_ge(pl["past"], c // 4 - 1)
                ins = pe.transpose(PS[6 + c // 4 % 2][:, (c % 4) * P:(c % 4) * P + NSEQ * BUF],
                                   PAST[0:NSEQ * BUF, c * P:(c + 1) * P], CP[0:NSEQ * BUF, 0:NSEQ * BUF])
                if c % 4 == 3:
                    ins.then_inc(pl["pastT"], 1)
            pe.wait_ge(ln["done"], 2 * KC)
            pe.wait_ge(pl["past"], 4)
            for q in range(4):
                if q >= 2:
                    pe.wait_ge(tr_ready, q - 1)
                for c in range(4):
                    ins = pe.transpose(PS[6 + q % 2][0:48, c * P:(c + 1) * P], X[:, 4 * q + c, T + 1 - 48:T + 1], IDN)
                ins.then_inc(pl["trT"], 1)
            pe.wait_ge(out_free, OUT["pool"] + 4)
            for j in range(4):
                pe.wait_ge(pl["lo"], j + 1)
                take_slab(SLAB["pool"] + j)
                for m in range(4):
                    o = OUT["pool"] + 4 * j + m
                    take_bank(o)
                    for k in range(4):
                        c = k * 512 + m * P
                        ins = three(PS[m][:, 0:T], WH[:, j % 2, c:c + P], WL[:, j % 2, c:c + P],
                                    MH[0][:, 4 * j + k, :], ML[0][:, 4 * j + k, :], k == 0, k == 3)
                    ins.then_inc(row_ready, 1)
                pe.drain().then_inc(slab_used, 1)
            layer_norm(2)
            ffn(1, 2)
            layer_norm(3)
            for q in range(4):
                pe.wait_ge(ln["done"], 3 * KC + 4 * q + 4)
                for a, n in enumerate((P, P, NS)):
                    z = 3 * q + a
                    if z >= 2:
                        pe.wait_ge(yrow_ready, z - 1)
                    for c in range(4):
                        ins = pe.transpose(PS[6 + z % 2][0:n, c * P:(c + 1) * P],
                                           X[:, 4 * q + c, 1 + a * P:1 + a * P + n], IDN)
                    ins.then_inc(yt["T"], 1)

        @block.scalar
        def _(act):
            def hi(q, j, s, n=2048, rows=P):
                act.wait_ge(raw_landed[j], 16 * (q + 1))
                act.wait_ge(slab_used, s + 1)
                act.activation(WH[0:rows, j % 2, 0:n], RAW[0:rows, j, 0:n], ACT.Copy).then_inc(hi_ready, 1)

            def mix_scale(name, c, b):
                act.wait_ge(mixlo_ready, MIX[name] * KC + c + 1)
                act.activation(TM[:, b, :], X[:, bass.ds(c, 1), 1:T + 1].rearrange("p a t -> p (a t)"), ACT.Copy,
                               scale=OMU[:, bass.ds(MU_ROW[name] * KC + c, 1)]).then_inc(tm_ready, 1)

            def mix_hi(name, c, b):
                q = MIX[name]
                act.wait_ge(mt_ready, q * KC + c + 1)
                act.activation(MH[q % 2][:, bass.ds(c, 1), :].rearrange("p a t -> p (a t)"),
                               K[:, c, :] if b is None else TM[:, b, :], ACT.Copy).then_inc(mixhi_ready, 1)

            def mix(name):
                for c in range(KC):
                    mix_hi(name, c, None)

            with act.Fori(0, 4) as i:
                for c in range(4):
                    act.wait_ge(x_turned, 8 + 4 * i + c + 1)
                    act.activation(X[:, bass.ds(4 * i + c, 1), 1:T + 1], PS[c][:, 0:T].rearrange("p (a t) -> p a t", a=1),
                                   ACT.Copy).then_inc(x_ready, 1)
            act.wait_ge(omu_ready, 1)
            act.wait_ge(x_ready, KC)
            widths = (KC * DL, KC * DL, 2048, 2048)
            for name, m in (("w", 0), ("a", 1), ("g", 2)):
                if m == 2:
                    act.wait_ge(slab_used, 2 + 1)
                if m < 2:
                    hi(0, m, m, widths[m])
                mix(name)

            def low_rank(j, rows, f):
                act.wait_ge(slab_used, 2 + j + 1)
                if j >= 2:
                    act.wait_ge(lhl_ready, j - 1)
                act.activation(TM[0:rows, j % 2, :], PS[j][0:rows, 0:T], f).then_inc(lh_ready, 1)
                act.wait_ge(lh_ready, j + 1)
                act.activation(LHH[0:rows, j, :], TM[0:rows, j % 2, :], ACT.Copy).then_inc(lhh_ready, 1)

            low_rank(0, DL, ACT.Tanh)
            hi(0, 2, 2)
            low_rank(1, DL, ACT.Copy)
            hi(0, 3, 3)
            low_rank(2, P, ACT.Sigmoid)
            hi(1, 0, 4)
            low_rank(3, P, ACT.Sigmoid)
            hi(1, 1, 5)
            mix("r")
            act.wait_ge(lhl_ready, 4)

            def square(name, evac, extra, n_next, rows_next=P, before=None):
                s0 = SLAB[name]

                def turn(i, last):
                    for j in range(4):
                        s = s0 + 4 * i + j + 2
                        if before is not None:
                            before(4 * i + j, j % 2)
                        if evac is not None:
                            evac(i, j, s0)
                        if not (last and j >= 2):
                            hi(s0 // 4 + i + (j + 2) // 4, (j + 2) % 4, s)
                        else:
                            hi(s0 // 4 + i + 1, (j + 2) % 4, s, n_next, rows_next)
                        if extra is not None:
                            extra(4 * i + j, j % 2)

                with act.Fori(0, 3) as i:
                    turn(i, False)
                turn(3, True)

            def keep(dst):
                def evac(i, j, s0):
                    act.wait_ge(slab_used, s0 + 4 * i + j + 3)
                    ins = act.activation(dst[:, bass.ds(4 * i + j, 1), :].rearrange("p a t -> p (a t)"), PS[j][:, 0:T],
                                         ACT.Copy)
                    ins.then_inc(out_free, 1)
                return evac

            def next_mix(name):
                def extra(c, b):
                    mix_scale(name, c, b)
                    mix_hi(name, c, b)
                return extra

            act.wait_ge(slab_used, 2 + SLAB["r"])
            square("r", keep(R), next_mix("k"), 2048)
            act.wait_ge(slab_used, 2 + SLAB["k"])
            square("k", keep(K), next_mix("v"), 2048)

            def key_squares(c, b):
                act.wait_ge(kk_ready, c + 1)
                act.wait_ge(kc_ready, c + 1)
                act.activation(TM[:, b, :], KK[:, bass.ds(c, 1), :].rearrange("p a t -> p (a t)"), ACT.Square)\
                   .then_inc(kks_ready, 1)

            def key_roots(c, b):
                act.wait_ge(kkn_ready, c + 1)
                act.activation(TM[:, b, :], PS[4 + b][:, 0:T], ACT.Sqrt).then_inc(kkd_ready, 1)

            square("v", keep(V), key_roots, 2048, DL, key_squares)

            for n, (dst, bias) in enumerate(((SG, "w0"), (A, "a0"))):
                with act.Fori(0, 4) as i:
                    for j in range(4):
                        act.wait_ge(row_ready, ROW["lora2"] + n * KC + 4 * i + j + 1)
                        act.activation(dst[:, bass.ds(4 * i + j, 1), :].rearrange("p a t -> p (a t)"), PS[j][:, 0:T],
                                       ACT.Sigmoid, bias=par(bias, 4 * i + j)).then_inc(out_free, 1)

            act.wait_ge(out_free, 4 + OUT["g2"])
            act.wait_ge(wkv_const, 16)
            hr = [slice(0, HN), slice(HN, P)]

            def flat(t):
                return t.rearrange("p a b -> p (a b)")

            def pair(z, p, i, part, done):
                B = z.B

                def await_step(steps, step, turn=0):
                    act.wait_ge(steps.sem, steps.value(step, i, turn))

                def norm(step):
                    if done is None:
                        return
                    if step == "sq":
                        act.wait_ge(z.ndve.sem, z.ndve.value("cen", done))
                        z.nact.done(act.activation(z.YT, one(R, chunk(z, done)), ACT.Square), "sq")
                    if step == "var":
                        act.wait_ge(z.npe.sem, z.npe.value("var", done))
                        z.nact.done(act.activation(z.YT, B[3][:, 0:T], ACT.Copy, bias=GN_EPS), "var")
                    if step == "sd":
                        act.wait_ge(z.nact.sem, z.nact.value("var", done))
                        z.nact.done(act.activation(z.YT, z.YT, ACT.Sqrt), "sd")

                if part == NORM:
                    yield
                    norm("sq")
                    yield
                    norm("var")
                    yield
                    norm("sd")
                    yield
                    yield
                    return

                if part == FRONT:
                    await_step(z.dve, "csx")
                    act.activation(z.PC[:, :], z.CS[:, :], ACT.Exp, scale=DECAY)
                    act.activation(z.CSX[:, :], z.CSX[:, :], ACT.Exp, scale=DECAY)
                    act.activation(z.VF[:, :], flat(V[:, bass.ds(p, 1), :]), ACT.Copy)
                    ins = act.activation(z.CS[:, :], z.CS[:, :], ACT.Exp, scale=-DECAY)
                    z.act.done(ins, "decays")
                    norm("sq")
                    yield
                    await_step(z.pe, "s0")
                    z.act.done(act.activation(flat(z.S0T[:, :, :]), B[0][:, :], ACT.Copy), "s0t")
                    norm("var")
                    yield
                    await_step(z.pe, "tok")
                    for t in range(2):
                        act.activation(flat(z.TOK[:, t, :, :]), B[1 + t][:, :], ACT.Copy)
                    z.act.done(act.activation(flat(z.TS[:, :, :]), B[3][:, 0:3 * HN], ACT.Copy), "tok")
                    norm("sd")
                    yield
                    yield
                    await_step(z.pe, "two")
                    act.activation(flat(z.TT[:, 0, :, :]), B[0][:, 0:256], ACT.Copy)
                    for h in range(2):
                        q = slice(h * HN, h * HN + 32)
                        ins = act.activation(z.STI[q, :], B[3][q, 0:NS], ACT.Copy)
                    z.act.done(ins, "two")
                    yield
                for lv in LEVELS[part]:
                    if lv == 1:
                        await_step(z.pe, "x1")
                        for h in range(2):
                            q = slice(h * HN, h * HN + 32)
                            act.activation(z.MVS[q, :], B[3][q, 128:128 + HN], ACT.Copy)
                        act.activation(z.WR[:, :, 4:8], z.AR[:, 1, SEQ:T].rearrange("p (b t) -> p b t", b=NSEQ), ACT.Copy)
                        z.act.done(act.activation(z.WR[:, :, 0:4],
                                                  B[3][:, 192:192 + NS].rearrange("p (b t) -> p b t", b=NSEQ),
                                                  ACT.Copy), "wr")
                    if lv == 4:
                        act.wait_ge(z.store_done, i + 1)
                        await_step(z.pe, "x4")
                        z.act.done(act.activation(flat(z.SOS[:, :, :]), B[0][:, :], ACT.Copy), "sos")
                    yield
                    if lv == 1:
                        await_step(z.pe, "t1")
                        z.act.done(act.activation(z.QT[:, :], B[3][:, 224:224 + NS], ACT.Copy), "qt")
                    if lv == 4:
                        await_step(z.pe, "t4")
                        z.act.done(act.activation(flat(z.MV[:, :, :]), B[3][:, 0:256], ACT.Copy), "mv")
                    yield
                if part == FRONT:
                    return
                await_step(z.pe, "q")
                for r in range(2):
                    act.activation(z.WT[:, :, r * CH:(r + 1) * CH],
                                   B[1 - r][:, 0:128].rearrange("p (t s) -> p t s", t=2), ACT.Copy)
                act.activation(z.U[0:CH, 0, :], B[2][0:CH, 0:P], ACT.Copy)
                z.act.done(act.activation(flat(z.Q[:, :, :]), B[2][:, 0:256], ACT.Copy), "q")
                yield
                yield
                for c in range(1, 4):
                    yield
                    yield
                await_step(z.pe, "y")
                z.act.done(act.activation(z.SOP[:, :], B[3][0:HN, 320:320 + P], ACT.Copy), "sop")
                yield

            turns(act, pair)
            for z in pairs:
                act.wait_ge(z.ndve.sem, z.ndve.value("done", KC // 2 - 1))
            act.wait_ge(wkv_done, 3)

            hi(13, 2, SLAB["g2"])
            hi(13, 3, SLAB["g2"] + 1)
            with act.Fori(0, KC) as c:
                act.wait_ge(yg_ready, c + 1)
                act.activation(MH[0][:, bass.ds(c, 1), :].rearrange("p a t -> p (a t)"),
                               R[:, bass.ds(c, 1), :].rearrange("p a t -> p (a t)"), ACT.Copy).then_inc(ygh_ready, 1)
            hi(14, 0, SLAB["o"])
            hi(14, 1, SLAB["o"] + 1)
            square("o", None, None, 2048)

            def layer_norm(k, halves):
                for q in range(4):
                    act.wait_ge(ln["cen"], 4 * k + q + 1)
                    if q == 0:
                        act.activation(LNS[:, 1, 0:1], IDN[:, 0:1], ACT.Sqrt)
                    act.activation(SQ[:, 4 * q:4 * q + 4, :], X[:, 4 * q:4 * q + 4, 1:T + 1], ACT.Square)\
                       .then_inc(ln["sq"], 1)
                act.wait_ge(ln["var"], k + 1)
                act.activation(LNS[:, 0, :], PS[5][:, 0:T], ACT.Copy, bias=LN_EPS).then_inc(ln["sd"], 1)
                act.wait_ge(ln["sd"], 2 * k + 1)
                act.activation(LNS[:, 0, :], LNS[:, 0, :], ACT.Sqrt).then_inc(ln["sd"], 1)
                with act.Fori(0, KC) as c:
                    act.wait_ge(ln["scaled"], k * KC + c + 1)
                    xc = X[:, bass.ds(c, 1), 1:T + 1].rearrange("p a t -> p (a t)")
                    if halves:
                        act.activation(MH[0][:, bass.ds(c, 1), :].rearrange("p a t -> p (a t)"), xc, ACT.Identity,
                                       bias=par("ln_b", k * KC + c))
                    act.activation(xc, xc, ACT.Identity, bias=par("ln_b", k * KC + c)).then_inc(ln["done"], 1)

            def ffn(layer, n_after):
                for g in range(2):
                    s0 = SLAB[f"ffn{layer}"] + g * FFN_SLABS
                    o0 = OUT[f"ffn{layer}"] + g * FFN_OUTS

                    def up(i, last):
                        for j in range(4):
                            hi(s0 // 4 + i + (j + 2) // 4, (j + 2) % 4, s0 + 4 * i + j + 2,
                               HH2 * P if last and j >= 2 else 2048)
                            if j % 2:
                                b = j // 2
                                hc = 2 * i + b
                                n = (2 * layer + g) * HG + hc
                                act.wait_ge(slab_used, s0 + 4 * i + j + 3)
                                act.wait_ge(hl_ready, n + 1)
                                act.activation(TM[:, b, :], PS[j - 1][:, 0:T], ACT.Sigmoid).then_inc(sg_ready, 1)
                                act.wait_ge(hid_ready, n + 1)
                                act.activation(HH[:, bass.ds(hc, 1), :].rearrange("p a t -> p (a t)"), TM[:, b, :],
                                               ACT.Copy).then_inc(hh_ready, 1)

                    with act.Fori(0, HG // 2 - 1) as i:
                        up(i, False)
                    up(HG // 2 - 1, True)
                    s1 = s0 + 2 * HG
                    with act.Fori(0, KC // 2 - 1) as i:
                        for j in range(4):
                            hi(s1 // 4 + i + (j + 2) // 4, (j + 2) % 4, s1 + 4 * i + j + 2, HH2 * P)
                    for j in range(4):
                        i = KC // 2 - 1
                        if j >= 2 and g == 1 and n_after == 0:
                            continue
                        hi(s1 // 4 + i + (j + 2) // 4, (j + 2) % 4, s1 + 4 * i + j + 2, HH2 * P if j < 2 else 2048)

            layer_norm(0, True)
            ffn(0, 2048)
            layer_norm(1, False)
            for q in range(4):
                act.wait_ge(pl["pastT"], q + 1)
                for c in range(4 * q, 4 * q + 4):
                    ins = act.activation(ES[0][:, c, :, 0:BUF],
                                         PS[6 + q % 2][:, (c % 4) * P:(c % 4) * P + NSEQ * BUF]
                                         .rearrange("p (b t) -> p b t", b=NSEQ), ACT.Copy)
                ins.then_inc(pl["past"], 1)
            for q in range(4):
                act.wait_ge(pl["trT"], q + 1)
                act.activation(TR[:, q * 512:(q + 1) * 512], PS[6 + q % 2][0:48, :], ACT.Copy).then_inc(tr_ready, 1)
            act.wait_ge(tr_ready, 4)
            act.dma_start(pool_p[0, 0], TR[1:16, :]).then_inc(tr_stored, 16)
            act.dma_start(pool_s[0][:, BUF - NSTEP:BUF, :], TR[16:48, :]).then_inc(tr_stored, 16)
            act.wait_ge(tr_stored, 32)
            for g in range(4):
                act.wait_ge(pl["d"], g + 1)
                act.activation(MH[0][:, 4 * g:4 * g + 4, :], DP[:, 4 * g:4 * g + 4, :], ACT.Copy)\
                   .then_inc(pl["hi"], 1)
            for j in range(4):
                q = SLAB["pool"] // 4 + (j + 2) // 4
                hi(q, (j + 2) % 4, SLAB["pool"] + j + 2)
                for m in range(4):
                    n = 4 * j + m
                    act.wait_ge(row_ready, ROW["pool"] + n + 1)
                    act.wait_ge(pl["scaled"], n + 1)
                    act.activation(TM[:, n % 2, :], PS[m][:, 0:T], ACT.Copy, scale=PAR[:, PCOL["scale"] + n:PCOL["scale"] + n + 1])\
                       .then_inc(out_free, 1)
            layer_norm(2, True)
            ffn(1, 0)
            layer_norm(3, False)

        @block.vector
        def _(dve):
            def lo(s, j, n=2048, rows=P):
                dve.wait_ge(hi_ready, s + 1)
                dve.tensor_tensor(WL[0:rows, j % 2, 0:n], RAW[0:rows, j, 0:n], WH[0:rows, j % 2, 0:n].bitcast(F32),
                                  ALU.subtract).then_inc(lo_ready, 1)

            def mix_add(name, c, b):
                mu = PAR[:, bass.ds(MU_ROW[name] * KC + c, 1)]
                dve.wait_ge(tm_ready, 4 + (MIX[name] - MIX["k"]) * KC + c + 1)
                dve.scalar_tensor_tensor(out=TM[:, b, 0:SEQ],
                                         in0=X[:, bass.ds(c, 1), 0:SEQ].rearrange("p a t -> p (a t)"), scalar=mu,
                                         in1=TM[:, b, 0:SEQ], op0=ALU.mult, op1=ALU.add)
                dve.scalar_tensor_tensor(out=TM[:, b, SEQ:T], in0=one(XPS, c), scalar=mu, in1=TM[:, b, SEQ:T],
                                         op0=ALU.mult, op1=ALU.add).then_inc(mt_ready, 1)

            def mix(name):
                q = MIX[name]
                for c in range(KC):
                    row = MU_ROW[name] * KC + c
                    if q:
                        dve.wait_ge(mixlo_ready, 2 + (q - 1) * KC + c + 1)
                    dve.scalar_tensor_tensor(out=K[:, c, :], in0=R[:, c, :], scalar=PAR[:, row:row + 1],
                                             in1=X[:, c, 1:T + 1], op0=ALU.mult, op1=ALU.add).then_inc(mt_ready, 1)

            def mix_lo(name, c, b):
                q = MIX[name]
                dve.wait_ge(mixhi_ready, q * KC + c + 1)
                dve.tensor_tensor(one(ML[q % 2], c), TM[:, b, :], one(MH[q % 2], c).bitcast(F32), ALU.subtract)\
                   .then_inc(mixlo_ready, 1)

            dve.wait_ge(par_turned, 1)
            dve.tensor_copy(PAR[:, 0:P + 96], PS[4][:, 0:P + 96])
            dve.tensor_copy(PAR[:, 256:384], PS[4][:, 256:384]).then_inc(par_ready, 1)
            dve.wait_ge(par_ready, 1)
            dve.tensor_scalar(OMU[:, :], PAR[:, 0:96], -1.0, 1.0, ALU.mult, ALU.add).then_inc(omu_ready, 1)
            dve.memset(X[:, :, 0:1], 0.0)
            with dve.Fori(0, 4) as i:
                for c in range(4):
                    dve.wait_ge(x_ready, 4 * i + c + 1)
                    dst = one(XPS, 4 * i + c).rearrange("p (b t) -> p b t", b=NSEQ)
                    dve.tensor_copy(dst[:, :, 0:1], PS[c][:, T:T + NSEQ].rearrange("p (b t) -> p b t", t=1))
                    dve.tensor_copy(dst[:, :, 1:NSTEP],
                                    PS[c][:, SEQ:T].rearrange("p (b t) -> p b t", b=NSEQ)[:, :, 0:NSTEP - 1])\
                       .then_inc(x_bank_free, 1)
            dve.wait_ge(x_bank_free, 4 + KC)
            for c in range(0, KC, 4):
                cs = slice(c, c + 4)
                dve.tensor_tensor(R[:, cs, 0:SEQ], X[:, cs, 0:SEQ], X[:, cs, 1:SEQ + 1], ALU.subtract)
                ins = dve.tensor_tensor(R[:, cs, SEQ:T], XPS[:, cs, :], X[:, cs, SEQ + 1:T + 1], ALU.subtract)
                ins.then_inc(tm_ready, 1)
            dve.wait_ge(tm_ready, 4)
            widths = (KC * DL, KC * DL, 2048, 2048)
            for name, m in (("w", 0), ("a", 1), ("g", 2)):
                if m < 2:
                    lo(m, m, widths[m])
                mix(name)

            def low_rank(j, rows):
                dve.wait_ge(lhh_ready, j + 1)
                dve.tensor_tensor(LHL[0:rows, j, :], TM[0:rows, j % 2, :], LHH[0:rows, j, :].bitcast(F32), ALU.subtract)\
                   .then_inc(lhl_ready, 1)
                dve.sem_inc(out_free, 1)

            low_rank(0, DL)
            lo(2, 2)
            low_rank(1, DL)
            lo(3, 3)
            low_rank(2, P)
            lo(4, 0)
            low_rank(3, P)
            lo(5, 1)
            mix("r")

            def square(name, evac, extra, n_next, rows_next=P, before=None):
                s0 = SLAB[name]

                def turn(i, last):
                    for j in range(4):
                        s = s0 + 4 * i + j + 2
                        if before is not None:
                            before(4 * i + j, j % 2)
                        if evac is not None:
                            evac(i, j, s0)
                        if not (last and j >= 2):
                            lo(s, (j + 2) % 4)
                        else:
                            lo(s, (j + 2) % 4, n_next, rows_next)
                        if extra is not None:
                            extra(4 * i + j, j % 2)

                with dve.Fori(0, 3) as i:
                    turn(i, False)
                turn(3, True)

            def next_mix(name):
                def extra(c, b):
                    mix_add(name, c, b)
                    mix_lo(name, c, b)
                return extra

            square("r", None, next_mix("k"), 2048)
            square("k", None, next_mix("v"), 2048)
            link = Chain(dve, kk_self, 2)

            def keys(c, b):
                dve.tensor_scalar(one(KK, c), one(K, c), par("k_k", c), None, ALU.mult).then_inc(kc_ready, 1)

            def unit_keys(c, b):
                link.turn(c)
                dve.wait_ge(kkd_ready, c + 1)
                link(dve.tensor_scalar(TM[:, b, :], TM[:, b, :], 1e-12, None, ALU.max))
                link(dve.reciprocal(TM[:, b, :], TM[:, b, :]))
                dve.tensor_tensor(one(KK, c), one(KK, c), TM[:, b, :], ALU.mult).then_inc(kk_ready, 1)

            dve.wait_ge(out_free, 4 + OUT["v"])
            square("v", None, unit_keys, 2048, DL, keys)
            dve.wait_ge(out_free, 4 + OUT["g2"])
            dve.wait_ge(kk_ready, 2 + KC)
            dve.wait_ge(lo_ready, 4 + SLAB["g2"])
            dve.sem_inc(wkv_go, 1)

            dve.wait_ge(wkv_const, 16)
            hr = [slice(0, HN), slice(HN, P)]

            def pair(z, p, i, part, done):
                B = z.B

                def await_step(steps, step, turn=0):
                    dve.wait_ge(steps.sem, steps.value(step, i, turn))

                def link(ins, step):
                    z.dve.done(ins, step)
                    await_step(z.dve, step)

                def norm(step):
                    if done is None:
                        return
                    c = chunk(z, done)
                    y = one(R, c)

                    def linked(ins, step):
                        z.ndve.done(ins, step)
                        dve.wait_ge(z.ndve.sem, z.ndve.value(step, done))

                    if step == "cen":
                        dve.wait_ge(z.npe.sem, z.npe.value("mean", done))
                        dve.wait_ge(z.dve.sem, z.dve.value("yout", done))
                        z.ndve.done(dve.tensor_tensor(y, y, B[2][:, 0:T], ALU.subtract), "cen")
                    if step == "rest":
                        dve.wait_ge(z.nact.sem, z.nact.value("sd", done))
                        linked(dve.reciprocal(z.YT, z.YT), "rstd")
                        linked(dve.tensor_tensor(y, y, z.YT, ALU.mult), "norm")
                        linked(dve.tensor_scalar(y, y, par("gn_g", c), par("gn_b", c), ALU.mult, ALU.add), "scale")
                        z.ndve.done(dve.tensor_tensor(y, y, one(SG, c), ALU.add), "done")

                if part == NORM:
                    norm("cen")
                    yield
                    yield
                    yield
                    yield
                    norm("rest")
                    yield
                    return

                def bcast(m, n):
                    return m.unsqueeze(1).broadcast_to([P, n, m.shape[1]])

                sg = one(SG, p)
                if part == FRONT:
                    link(dve.tensor_tensor_scan(z.CS[:, :], NOTSTART, sg, 0.0, ALU.mult, ALU.add), "cs")
                    z.dve.done(dve.tensor_tensor(z.CSX[:, :], z.CS[:, :], sg, ALU.subtract), "csx")
                    norm("cen")
                    link(dve.tensor_scalar(z.KF[:, :], one(A, p), -1.0, par("k_a", p), ALU.add, ALU.mult), "kt")
                    link(dve.scalar_tensor_tensor(out=z.KF[:, :], in0=z.KF[:, :], scalar=1.0, in1=one(K, p), op0=ALU.add,
                                                  op1=ALU.mult), "kt2")
                    z.dve.done(dve.tensor_tensor(z.BF[:, :], one(KK, p), one(A, p), ALU.mult), "bfa")
                    link(dve.scalar_tensor_tensor(out=sg, in0=one(R, p), scalar=par("r_k", p), in1=z.KF[:, :],
                                                  op0=ALU.mult, op1=ALU.mult), "rkp")
                    yield
                    await_step(z.act, "decays")
                    dve.scalar_tensor_tensor(out=z.AR[:, 0, :], in0=one(KK, p), scalar=-1.0, in1=z.CSX[:, :], op0=ALU.mult,
                                             op1=ALU.mult)
                    dve.tensor_tensor(z.AR[:, 1, :], one(R, p), z.PC[:, :], ALU.mult)
                    dve.tensor_tensor(z.BF[:, :], z.BF[:, :], z.CS[:, :], ALU.mult)
                    z.dve.done(dve.tensor_tensor(z.KF[:, :], z.KF[:, :], z.CS[:, :], ALU.mult), "feats")
                    yield
                    yield
                    await_step(z.pe, "prod")
                    for h in range(2):
                        dve.tensor_tensor(z.LT[:, h:4:2, :], B[3 * h][:, 256:384].rearrange("p (t s) -> p t s", t=2),
                                          bcast(M_CHUNK, 2), ALU.mult)
                    link(dve.tensor_tensor(z.SM[:, :], B[0][:, 384:448], MS_PROD, ALU.mult), "sm")
                    link(dve.tensor_tensor(z.TT[:, 1, :, :], z.LT[:, :, :], bcast(M_ONE, 4), ALU.mult), "tit")
                    link(dve.tensor_tensor(z.STT[:, :], z.SM[:, 0:NS], MS_ONE, ALU.mult), "stt")
                    dve.tensor_tensor(z.TT[:, 1, :, :], z.TT[:, 1, :, :], bcast(IDC, 4), ALU.add)
                    for h in range(2):
                        dve.tensor_tensor(z.RB[:, :, h, :], B[3 * h][:, 0:256].rearrange("p (t s) -> p t s", t=2),
                                          bcast(M_PROD[:, P:2 * P], 2), ALU.mult)
                    z.dve.done(dve.tensor_tensor(z.STT[:, :], z.STT[:, :], IDS, ALU.add), "two")
                    for h in range(2):
                        ins = dve.tensor_tensor(z.MR[:, :, h, :], B[1 + h][:, :].rearrange("p (t n) -> p t n", t=2),
                                                bcast(M_PROD, 2), ALU.mult)
                    z.dve.done(ins, "masks")
                    yield
                    norm("rest")
                    yield
                was = B[0][:, 0:64].rearrange("p (b n) -> p b n", b=NSEQ)
                seqs = lambda t: t.rearrange("p (b t) -> p b t", b=NSEQ)
                for lv in LEVELS[part]:
                    await_step(z.pe, f"x{lv}")
                    if lv == 0:
                        for h in range(2):
                            q = slice(h * HN, h * HN + 32)
                            dve.tensor_tensor(z.SXL[q, :], B[3][q, 64:64 + NS], MS_TWO[q, :], ALU.mult)
                    if lv == 2:
                        await_step(z.act, "qt")
                        dve.tensor_tensor(seqs(z.UT[:, :]), was[:, :, 0:4], seqs(z.QT[:, :]), ALU.add)
                        dve.tensor_copy(seqs(z.YS[:, :]), was[:, :, 4:8])
                    z.dve.done(dve.tensor_tensor(z.XL[:, :, :], B[1][:, 0:256].rearrange("p (u t) -> p u t", u=4),
                                                 bcast(M_LEVEL[lv], 4), ALU.mult), f"x{lv}")
                    yield
                    await_step(z.pe, f"t{lv}")
                    if lv == 0:
                        for h in range(2):
                            q = slice(h * HN, h * HN + 32)
                            dve.tensor_tensor(z.STT[q, :], B[3][q, 96:96 + NS], z.STT[q, :], ALU.add)
                    if lv < 4:
                        ins = dve.tensor_tensor(z.TT[:, :, :, :].rearrange("p n u t -> p (n u t)"), B[2][:, :],
                                                z.TT[:, :, :, :].rearrange("p n u t -> p (n u t)"), ALU.add)
                    else:
                        ins = dve.tensor_tensor(z.TT[:, 1, :, :].rearrange("p u t -> p (u t)"), B[2][:, 256:512],
                                                z.TT[:, 1, :, :].rearrange("p u t -> p (u t)"), ALU.add)
                    z.dve.done(ins, f"t{lv}")
                    if lv == 2:
                        for h in range(2):
                            q = slice(h * HN, h * HN + 32)
                            ins = dve.tensor_copy(z.TS[q, 2, :], B[3][q, 256:256 + HN])
                        link(ins, "utc")
                        z.dve.done(dve.tensor_tensor(z.UVX[:, :, :], bcast(z.TS[:, 2, :], NSEQ),
                                                     MS_SEQ.unsqueeze(2).broadcast_to([P, NSEQ, HN]), ALU.mult), "uvx")
                    if lv == 3:
                        link(dve.tensor_tensor(z.UVX[:, :, :], B[0][:, :].rearrange("p (b v) -> p b v", b=NSEQ),
                                               z.S0T[:, :, :], ALU.add), "snw")
                        ends = seqs(z.PC[:, SEQ:T])[:, :, NSTEP - 1:NSTEP]
                        z.dve.done(dve.tensor_tensor(z.UVX[:, :, :], z.UVX[:, :, :],
                                                     ends.broadcast_to([P, NSEQ, HN]), ALU.mult), "snw2")
                    yield
                if part == FRONT:
                    return
                await_step(z.act, "q")
                z.dve.done(dve.tensor_tensor(one(SG, p), B[1][:, 128:128 + T], one(V, p), ALU.mult), "bonv")
                yield
                await_step(z.pe, "s0c")
                z.dve.done(dve.tensor_scalar(z.ST[:, 1, :], B[3][:, 256:256 + HN], z.PC[:, CH - 1:CH], None, ALU.mult),
                           "st0")
                yield
                for c in range(1, 4):
                    t, r = c // 2, c % 2
                    rr = hr[r]
                    end = z.PC[:, (c + 1) * CH - 1:(c + 1) * CH]
                    await_step(z.dve, f"st{c - 1}")
                    z.dve.done(dve.tensor_scalar(z.SPD[:, :], z.ST[:, r, :], end, None, ALU.mult), f"spd{c}")
                    await_step(z.pe, f"u{c}")
                    for h in range(2):
                        ins = dve.tensor_tensor(z.U[rr, t, hr[h]], B[1 + h][rr, 448:512], z.Q[rr, 2 * t + h, :], ALU.add)
                    z.dve.done(ins, f"u{c}")
                    yield
                    await_step(z.pe, f"s{c}")
                    await_step(z.dve, f"spd{c}")
                    z.dve.done(dve.scalar_tensor_tensor(out=z.ST[:, (c + 1) % 2, :], in0=B[3][:, 256:256 + HN],
                                                        scalar=end, in1=z.SPD[:, :], op0=ALU.mult, op1=ALU.add),
                               f"st{c}")
                    yield
                await_step(z.pe, "y")
                z.dve.done(dve.tensor_scalar(one(R, p)[:, 0:SEQ], B[0][:, 128:384], 1.0, None, ALU.mult), "yr")
                z.dve.done(dve.tensor_tensor(one(R, p)[:, SEQ:T], B[0][:, 384:384 + NS], z.YS[:, :], ALU.add), "yout")
                yield

            turns(dve, pair)
            for z in pairs:
                dve.wait_ge(z.ndve.sem, z.ndve.value("done", KC // 2 - 1))
            dve.sem_inc(wkv_done, 1)

            lo(SLAB["g2"], 2)
            lo(SLAB["g2"] + 1, 3)
            with dve.Fori(0, 4) as i:
                for j in range(4):
                    c = 4 * i + j
                    dve.wait_ge(row_ready, ROW["g2"] + c + 1)
                    dve.tensor_tensor(one(R, c), PS[j][:, 0:T], one(R, c), ALU.mult).then_inc(yg_ready, 1)
                    dve.wait_ge(ygh_ready, c + 1)
                    dve.sem_inc(out_free, 1)
                    dve.tensor_tensor(one(ML[0], c), one(R, c), one(MH[0], c).bitcast(F32), ALU.subtract)\
                       .then_inc(ygl_ready, 1)
            lo(SLAB["o"], 0)
            lo(SLAB["o"] + 1, 1)

            def xcur(c):
                return X[:, bass.ds(c, 1), 1:T + 1].rearrange("p a t -> p (a t)")

            def residual(i, j, s0):
                dve.wait_ge(slab_used, s0 + 4 * i + j + 3)
                dve.scalar_tensor_tensor(out=xcur(4 * i + j), in0=xcur(4 * i + j), scalar=ALPHA, in1=PS[j][:, 0:T],
                                         op0=ALU.mult, op1=ALU.add).then_inc(out_free, 1)

            dve.wait_ge(xback, 16)
            square("o", residual, None, 2048)

            def layer_norm(k, halves):
                dve.wait_ge(ln["mean"], k + 1)
                for q in range(4):
                    xs = X[:, 4 * q:4 * q + 4, 1:T + 1]
                    dve.tensor_tensor(xs, xs, PS[4][:, 0:T].unsqueeze(1).broadcast_to([P, 4, T]), ALU.subtract)\
                       .then_inc(ln["cen"], 1)
                dve.wait_ge(ln["sd"], 2 * k + 2)
                dve.reciprocal(LNS[:, 1, :], LNS[:, 0, :]).then_inc(ln["rstd"], 1)
                dve.wait_ge(ln["rstd"], k + 1)
                dve.wait_ge(ln["cen"], 4 * k + 4)

                def scaled(c):
                    dve.scalar_tensor_tensor(out=xcur(c), in0=xcur(c), scalar=par("ln_g", k * KC + c),
                                             in1=LNS[:, 1, :], op0=ALU.mult, op1=ALU.mult).then_inc(ln["scaled"], 1)

                def low(c):
                    dve.wait_ge(ln["done"], k * KC + c + 1)
                    dve.tensor_tensor(one(ML[0], c), xcur(c), one(MH[0], c).bitcast(F32), ALU.subtract)\
                       .then_inc(ln["lo"], 1)

                if not halves:
                    with dve.Fori(0, KC) as c:
                        scaled(c)
                    return
                for c in range(3):
                    scaled(c)
                with dve.Fori(0, KC - 3) as c:
                    scaled(c + 3)
                    low(c)
                for c in range(KC - 3, KC):
                    low(c)

            def ffn(layer, n_after):
                for g in range(2):
                    s0 = SLAB[f"ffn{layer}"] + g * FFN_SLABS
                    o0 = OUT[f"ffn{layer}"] + g * FFN_OUTS

                    def up(i, last):
                        for j in range(4):
                            lo(s0 + 4 * i + j + 2, (j + 2) % 4, HH2 * P if last and j >= 2 else 2048)
                            if j % 2:
                                b = j // 2
                                hc = 2 * i + b
                                n = (2 * layer + g) * HG + hc
                                dve.wait_ge(sg_ready, n + 1)
                                dve.tensor_tensor(TM[:, b, :], TM[:, b, :], PS[j - 1][:, 0:T], ALU.mult)\
                                   .then_inc(hid_self, 1)
                                dve.wait_ge(hid_self, n + 1)
                                dve.tensor_tensor(TM[:, b, :], TM[:, b, :], PS[j][:, 0:T], ALU.mult)\
                                   .then_inc(hid_ready, 1)
                                dve.wait_ge(hid_ready, n + 1)
                                dve.sem_inc(out_free, 2)
                                dve.wait_ge(hh_ready, n + 1)
                                dve.tensor_tensor(one(HL, hc), TM[:, b, :], one(HH, hc).bitcast(F32), ALU.subtract)\
                                   .then_inc(hl_ready, 1)

                    with dve.Fori(0, HG // 2 - 1) as i:
                        up(i, False)
                    up(HG // 2 - 1, True)
                    s1, o1 = s0 + 2 * HG, o0 + 2 * HG

                    def down(i, j):
                        c = 2 * i + j // 2
                        dve.wait_ge(slab_used, s1 + 4 * i + j + 3)
                        if g == 0:
                            ins = dve.scalar_tensor_tensor(out=xcur(c), in0=xcur(c), scalar=ALPHA,
                                                           in1=PS[j // 2][:, 0:T], op0=ALU.mult, op1=ALU.add)
                        else:
                            ins = dve.tensor_tensor(xcur(c), xcur(c), PS[j // 2][:, 0:T], ALU.add)
                        ins.then_inc(out_free, 1)

                    with dve.Fori(0, KC // 2 - 1) as i:
                        for j in range(4):
                            if j % 2:
                                down(i, j)
                            lo(s1 + 4 * i + j + 2, (j + 2) % 4, HH2 * P)
                    for j in range(4):
                        i = KC // 2 - 1
                        if j % 2:
                            down(i, j)
                        if not (j >= 2 and g == 1 and n_after == 0):
                            lo(s1 + 4 * i + j + 2, (j + 2) % 4, HH2 * P if j < 2 else 2048)

            layer_norm(0, True)
            ffn(0, 2048)
            dve.wait_ge(out_free, 4 + OUT["pool"])
            dve.sem_inc(past_go, 2)
            layer_norm(1, False)
            dve.wait_ge(ln["done"], 2 * KC)
            link = Chain(dve, pl["self"])
            dve.memset(EP[1][:, :, 0:BUF], 0.0)
            dve.memset(X[:, :, 0:1], 0.0).then_inc(pl["ext"], 1)
            dve.wait_ge(pl["ext"], 1)
            dve.wait_ge(pl["pastT"], 4)
            dve.wait_ge(inv_in, 16)

            def low(g):
                gs = slice(4 * g, 4 * g + 4)
                dve.wait_ge(pl["hi"], g + 1)
                dve.tensor_tensor(ML[0][:, gs, :], DP[:, gs, :], MH[0][:, gs, :].bitcast(F32), ALU.subtract)\
                   .then_inc(pl["lo"], 1)

            for lv in range(4):
                d, f = 1 << lv, 4 * lv
                a, b = lv % 2, (lv + 1) % 2
                m = (2 << lv) - 1
                if lv == 0:
                    link(dve.tensor_tensor(EP[1][:, 0:4, BUF:], X[:, 0:4, 1:SEQ + 1], X[:, 0:4, 0:SEQ], ALU.add))
                else:
                    link(dve.tensor_tensor(EP[b][:, f:KC, m:], EP[a][:, f:KC, m:], EP[a][:, f:KC, m - d:BUF + SEQ - d],
                                           ALU.add))
                win = 2 << lv
                gs = slice(4 * lv, 4 * lv + 4)
                link(dve.tensor_tensor(EP[b][:, gs, BUF:BUF + 16], EP[b][:, gs, BUF:BUF + 16],
                                       CI[:, lv, :].unsqueeze(1).broadcast_to([P, 4, 16]), ALU.mult))
                dve.scalar_tensor_tensor(out=DP[:, gs, 0:SEQ], in0=EP[b][:, gs, BUF:], scalar=1.0 / win,
                                         in1=X[:, gs, 1:SEQ + 1], op0=ALU.mult, op1=ALU.subtract)
                if lv == 0:
                    link(dve.tensor_tensor(EP[1][:, 4:KC, BUF:], X[:, 4:KC, 1:SEQ + 1], X[:, 4:KC, 0:SEQ], ALU.add))
                dve.wait_ge(pl["es"], lv + 4 if lv else 2)
                for c in range(4 * lv, 4 * lv + 4):
                    ins = dve.scalar_tensor_tensor(
                        out=DP[:, c, SEQ:T].rearrange("p (b t) -> p b t", b=NSEQ), in0=ES[b][:, c, :, BUF:],
                        scalar=1.0 / win, in1=X[:, c, SEQ + 1:T + 1].rearrange("p (b t) -> p b t", b=NSEQ),
                        op0=ALU.mult, op1=ALU.subtract)
                ins.then_inc(pl["d"], 1)
                if lv:
                    low(lv - 1)
            low(3)
            dve.sem_inc(pl["scaled"], 2)
            for j in range(4):
                lo(SLAB["pool"] + j + 2, (j + 2) % 4)
                for m in range(4):
                    n = 4 * j + m
                    dve.wait_ge(out_free, 4 + OUT["pool"] + n + 1)
                    dve.scalar_tensor_tensor(out=X[:, n, 1:T + 1], in0=X[:, n, 1:T + 1], scalar=ALPHA,
                                             in1=TM[:, n % 2, :], op0=ALU.mult, op1=ALU.add).then_inc(pl["scaled"], 1)
            dve.wait_ge(pl["scaled"], 2 + KC)
            layer_norm(2, True)
            ffn(1, 0)
            layer_norm(3, False)
            for q in range(4):
                for a, n in enumerate((P, P, NS)):
                    z = 3 * q + a
                    dve.wait_ge(yt["T"], z + 1)
                    dve.tensor_copy(YROW[0:n, a, q * 512:(q + 1) * 512], PS[6 + z % 2][0:n, :]).then_inc(yrow_ready, 1)


_INS = ["x_prompt", "x_sample", "state_wkv", "state_shift", "state_pool", "ln_g", "ln_b", "rw_mu", "rw_wr", "rw_wk",
        "rw_wv", "rw_wo", "rw_w0", "rw_w1", "rw_w2", "rw_a0", "rw_a1", "rw_a2", "rw_g1", "rw_g2", "rw_kk", "rw_ka",
        "rw_rk", "rw_gn_g", "rw_gn_b", "pool_w", "pool_scale", "ffn_w_in", "ffn_w_down"]
_OUTS = [(1, SEQ, D), (NSEQ, NSTEP, D), (1, 1, H, HN, HN), (1, 1, D), (1, 1, BUF, D), (1, NSEQ, H, HN, HN),
         (1, NSEQ, D), (1, NSEQ, BUF, D)]


def kernel(**inputs):
    import concourse.bacc as _bacc
    from concourse import mybir as _mybir
    from concourse.bass_utils import run_bass_kernel_spmd as _run

    nc = _bacc.Bacc("TRN2", target_bir_lowering=False, num_devices=1)
    arrays, args = {}, []
    given = [(n, np.ascontiguousarray(inputs[n])) for n in _INS]
    given += list(zip(("c_perm", "c_wkv", "c_inv"), shape_constants()))
    for name, a in given:
        arrays[f"in_{name}"] = a
        args.append(nc.dram_tensor(f"in_{name}", a.shape, _mybir.dt.from_np(a.dtype), kind="ExternalInput").ap())
    for i, shape in enumerate(_OUTS):
        args.append(nc.dram_tensor(f"out_{i}", shape, F32, kind="ExternalOutput").ap())
    build(nc, *args)
    r = _run(nc, [arrays], core_ids=[0])
    return tuple(r.results[0][f"out_{i}"] for i in range(len(_OUTS)))
```
